# Optimizing a Trainium2 kernel written in Bass

```python
import jax
import jax.numpy as jnp
from jax import lax
import numpy as np

D_MODEL = 1024
BATCH = 1
SEQ = 1024
DEPTH = 2

GRID_W = 64
CTX_LEN = 256
RET_HEADS = 8
RET_DK = 64
RET_DV = 64
QK_WIDTH = RET_HEADS * RET_DK
RET_WIDTH = RET_HEADS * RET_DV
CONV_CH = 512
CONV_WIDTH = 31
MIX_WIDTH = RET_WIDTH + CONV_CH
D_FF = 4 * D_MODEL
CHUNK = 128
ROPE_BASE = 10000.0
LN_EPS = 1e-5
DEEPNORM_ALPHA = (2 * DEPTH) ** 0.25
DEEPNORM_BETA = (8 * DEPTH) ** -0.25
Q_OFF = 0
K_OFF = Q_OFF + QK_WIDTH
V_OFF = K_OFF + QK_WIDTH
G_OFF = V_OFF + RET_WIDTH
A_OFF = G_OFF + RET_WIDTH
B_OFF = A_OFF + CONV_CH
IN_WIDTH = B_OFF + CONV_CH

kernel_name = 'hybrid_retention_conformer_dit'

def layer_norm(x, w, b):
    xf = x.astype(jnp.float32)
    mu = jnp.mean(xf, axis=-1, keepdims=True)
    var = jnp.mean(jnp.square(xf - mu), axis=-1, keepdims=True)
    y = (xf - mu) * lax.rsqrt(var + LN_EPS)
    return (y * w.astype(jnp.float32) + b.astype(jnp.float32)).astype(x.dtype)

def modulate(h, shift, scale):
    return h * (1.0 + scale) + shift

def adaln(cond, w_ada, b_ada):
    return jnp.split(jax.nn.silu(cond) @ w_ada + b_ada, 6, axis=-1)

def rope_tables(n):
    rows = n // GRID_W
    row = jnp.repeat(jnp.arange(rows, dtype=jnp.float32), GRID_W)
    col = jnp.tile(jnp.arange(GRID_W, dtype=jnp.float32), rows)
    n_freq = RET_DK // 4
    inv = ROPE_BASE ** (-jnp.arange(n_freq, dtype=jnp.float32) / n_freq)
    ang = jnp.concatenate([row[:, None] * inv, col[:, None] * inv], axis=-1)
    return jnp.cos(ang), jnp.sin(ang)

def apply_rope(t, cos, sin):
    c = cos.astype(t.dtype)
    s = sin.astype(t.dtype)
    t1 = t[..., 0::2]
    t2 = t[..., 1::2]
    return jnp.stack([t1 * c - t2 * s, t1 * s + t2 * c], axis=-1).reshape(t.shape)

def split_heads(t, d):
    b, n, _ = t.shape
    return t.reshape(b, n, RET_HEADS, d).transpose(0, 2, 1, 3)

def flip_seq(t):
    return t[:, :, ::-1]

def retention_scan(q, k, v, log_gamma, s0):
    b, h, n, _ = q.shape
    dv = v.shape[-1]
    nc = n // CHUNK
    lg = log_gamma.astype(jnp.float32)[:, None]
    idx = jnp.arange(CHUNK, dtype=jnp.float32)
    diff = idx[:, None] - idx[None, :]
    intra = jnp.where(diff >= 0, jnp.exp(lg[:, :, None] * jnp.maximum(diff, 0.0)), 0.0)
    q_dec = jnp.exp(lg * (idx + 1.0))
    k_dec = jnp.exp(lg * (CHUNK - 1.0 - idx))
    c_dec = jnp.exp(lg * CHUNK)

    def chunks(t):
        return t.astype(jnp.float32).reshape(b, h, nc, CHUNK, t.shape[-1]).transpose(2, 0, 1, 3, 4)

    def step(s, qkv):
        qc, kc, vc = qkv
        scores = jnp.einsum('bhid,bhjd->bhij', qc, kc) * intra
        o = (jnp.einsum('bhij,bhjv->bhiv', scores, vc)
             + jnp.einsum('bhid,bhdv->bhiv', qc * q_dec[..., None], s))
        s = s * c_dec[..., None] + jnp.einsum('bhjd,bhjv->bhdv', kc * k_dec[..., None], vc)
        return s, o

    s_fin, o = lax.scan(step, s0.astype(jnp.float32), (chunks(q), chunks(k), chunks(v)))
    return o.transpose(1, 2, 0, 3, 4).reshape(b, h, n, dv), s_fin

def final_state(k, v, log_gamma):
    length = k.shape[2]
    lg = log_gamma.astype(jnp.float32)[:, None]
    w = jnp.exp(lg * (length - 1.0 - jnp.arange(length, dtype=jnp.float32)))
    return jnp.einsum('bhjd,bhjv->bhdv', k.astype(jnp.float32) * w[..., None], v.astype(jnp.float32))

def retention_readout(o, g, gn_w, gn_b):
    mu = jnp.mean(o, axis=-1, keepdims=True)
    var = jnp.mean(jnp.square(o - mu), axis=-1, keepdims=True)
    on = (o - mu) * lax.rsqrt(var + LN_EPS)
    b, h, n, dv = on.shape
    on = on.transpose(0, 2, 1, 3).reshape(b, n, h * dv)
    on = (on * gn_w.astype(jnp.float32) + gn_b.astype(jnp.float32)).astype(g.dtype)
    return jax.nn.silu(g) * on

def conformer_conv(a, gate, conv_w, conv_b, ln_w, ln_b):
    u = a * jax.nn.sigmoid(gate)
    u = lax.conv_general_dilated(
        u, conv_w[:, None, :], window_strides=(1,),
        padding=[(CONV_WIDTH // 2, CONV_WIDTH // 2)],
        dimension_numbers=('NWC', 'WIO', 'NWC'),
        feature_group_count=CONV_CH) + conv_b
    return jax.nn.silu(layer_norm(u, ln_w, ln_b))

def mixer_output(o_ret, p, gn_w, gn_b, conv_w, conv_b, cln_w, cln_b, w_out):
    ret = retention_readout(o_ret, p[..., G_OFF:A_OFF], gn_w, gn_b)
    conv = conformer_conv(p[..., A_OFF:B_OFF], p[..., B_OFF:IN_WIDTH], conv_w, conv_b, cln_w, cln_b)
    return jnp.concatenate([ret, conv], axis=-1) @ w_out

def mlp_sublayer(h, shift, scale, gate, w1, w2, ln_w, ln_b):
    y = jnp.square(jax.nn.relu(modulate(h, shift, scale) @ w1)) @ w2
    return layer_norm(DEEPNORM_ALPHA * h + gate * y, ln_w, ln_b)

def setup_inputs(seed: int = 0) -> dict:
    key = jax.random.key(seed)
    ks = jax.random.split(key, 22)
    f32 = jnp.float32

    def nrm(k, shape, s):
        return jax.random.normal(k, shape, f32) * s

    base_rate = jnp.log(-jnp.log1p(-(2.0 ** (-5.0 - jnp.arange(RET_HEADS, dtype=f32)))))
    v_scale = jnp.ones((IN_WIDTH,), f32).at[V_OFF:G_OFF].set(DEEPNORM_BETA)
    return {
        'x': nrm(ks[0], (BATCH, SEQ, D_MODEL), 1.0),
        'c': nrm(ks[1], (BATCH, D_MODEL), 1.0),
        'ctx': nrm(ks[2], (BATCH, CTX_LEN, D_MODEL), 1.0),
        'c_ctx': nrm(ks[3], (D_MODEL,), 1.0),
        'w_ada': nrm(ks[4], (DEPTH, D_MODEL, 6 * D_MODEL), 0.5 * D_MODEL ** -0.5),
        'b_ada': nrm(ks[5], (DEPTH, 6 * D_MODEL), 0.01),
        'w_in': nrm(ks[6], (DEPTH, D_MODEL, IN_WIDTH), D_MODEL ** -0.5) * v_scale,
        'ret_log_rate_fwd': base_rate + nrm(ks[7], (DEPTH, RET_HEADS), 0.1),
        'ret_log_rate_bwd': base_rate + nrm(ks[8], (DEPTH, RET_HEADS), 0.1),
        'ret_gn_w': 1.0 + nrm(ks[9], (DEPTH, RET_WIDTH), 0.02),
        'ret_gn_b': nrm(ks[10], (DEPTH, RET_WIDTH), 0.02),
        'conv_w': nrm(ks[11], (DEPTH, CONV_WIDTH, CONV_CH), CONV_WIDTH ** -0.5),
        'conv_b': nrm(ks[12], (DEPTH, CONV_CH), 0.02),
        'conv_ln_w': 1.0 + nrm(ks[13], (DEPTH, CONV_CH), 0.02),
        'conv_ln_b': nrm(ks[14], (DEPTH, CONV_CH), 0.02),
        'w_out': nrm(ks[15], (DEPTH, MIX_WIDTH, D_MODEL), DEEPNORM_BETA * MIX_WIDTH ** -0.5),
        'ln1_w': 1.0 + nrm(ks[16], (DEPTH, D_MODEL), 0.02),
        'ln1_b': nrm(ks[17], (DEPTH, D_MODEL), 0.02),
        'w_ff1': nrm(ks[18], (DEPTH, D_MODEL, D_FF), D_MODEL ** -0.5),
        'w_ff2': nrm(ks[19], (DEPTH, D_FF, D_MODEL), DEEPNORM_BETA * D_FF ** -0.5),
        'ln2_w': 1.0 + nrm(ks[20], (DEPTH, D_MODEL), 0.02),
        'ln2_b': nrm(ks[21], (DEPTH, D_MODEL), 0.02),
    }

def reference(x, c, ctx, c_ctx, w_ada, b_ada, w_in, ret_log_rate_fwd, ret_log_rate_bwd,
              ret_gn_w, ret_gn_b, conv_w, conv_b, conv_ln_w, conv_ln_b, w_out,
              ln1_w, ln1_b, w_ff1, w_ff2, ln2_w, ln2_b):
    n = x.shape[1]
    cos, sin = rope_tables(n)
    zero_state = jnp.zeros((x.shape[0], RET_HEADS, RET_DK, RET_DV), jnp.float32)

    for l in range(DEPTH):
        last = l == DEPTH - 1
        sh1, sc1, g1, sh2, sc2, g2 = [t[:, None, :] for t in adaln(c, w_ada[l], b_ada[l])]
        csh1, csc1, cg1, csh2, csc2, cg2 = adaln(c_ctx, w_ada[l], b_ada[l])
        lg_f = -jnp.exp(ret_log_rate_fwd[l])
        lg_b = -jnp.exp(ret_log_rate_bwd[l])

        hc = modulate(ctx, csh1, csc1)
        if last:
            pkv = hc @ w_in[l][:, K_OFF:G_OFF]
            kc = split_heads(pkv[..., :QK_WIDTH], RET_DK)
            vc = split_heads(pkv[..., QK_WIDTH:], RET_DV)
            s_f = final_state(kc, vc, lg_f)
            s_b = final_state(flip_seq(kc), flip_seq(vc), lg_b)
        else:
            pc = hc @ w_in[l]
            qc = split_heads(pc[..., Q_OFF:K_OFF], RET_DK)
            kc = split_heads(pc[..., K_OFF:V_OFF], RET_DK) * (RET_DK ** -0.5)
            vc = split_heads(pc[..., V_OFF:G_OFF], RET_DV)
            oc_f, s_f = retention_scan(qc, kc, vc, lg_f, zero_state)
            oc_b, s_b = retention_scan(flip_seq(qc), flip_seq(kc), flip_seq(vc), lg_b, zero_state)
            mix_c = mixer_output(oc_f + flip_seq(oc_b), pc, ret_gn_w[l], ret_gn_b[l],
                                 conv_w[l], conv_b[l], conv_ln_w[l], conv_ln_b[l], w_out[l])

        p = modulate(x, sh1, sc1) @ w_in[l]
        q = apply_rope(split_heads(p[..., Q_OFF:K_OFF], RET_DK), cos, sin)
        k = apply_rope(split_heads(p[..., K_OFF:V_OFF], RET_DK), cos, sin) * (RET_DK ** -0.5)
        v = split_heads(p[..., V_OFF:G_OFF], RET_DV)
        o_f, _ = retention_scan(q, k, v, lg_f, s_f)
        o_b, _ = retention_scan(flip_seq(q), flip_seq(k), flip_seq(v), lg_b, s_b)
        mix_x = mixer_output(o_f + flip_seq(o_b), p, ret_gn_w[l], ret_gn_b[l],
                             conv_w[l], conv_b[l], conv_ln_w[l], conv_ln_b[l], w_out[l])
        x = layer_norm(DEEPNORM_ALPHA * x + g1 * mix_x, ln1_w[l], ln1_b[l])
        x = mlp_sublayer(x, sh2, sc2, g2, w_ff1[l], w_ff2[l], ln2_w[l], ln2_b[l])

        if not last:
            ctx = layer_norm(DEEPNORM_ALPHA * ctx + cg1 * mix_c, ln1_w[l], ln1_b[l])
            ctx = mlp_sublayer(ctx, csh2, csc2, cg2, w_ff1[l], w_ff2[l], ln2_w[l], ln2_b[l])

    return x


_drawn_inputs = setup_inputs


def setup_inputs(seed=0):
    import zlib

    import numpy as np

    out = dict(_drawn_inputs(seed))
    spreads = {}
    factors = {'b_ada': 6.312,
     'ret_log_rate_fwd': 22.648,
     'ret_log_rate_bwd': 22.712,
     'ret_gn_w': 41.925,
     'ret_gn_b': 41.938,
     'conv_b': 8.0,
     'conv_ln_w': 34.129,
     'conv_ln_b': 34.402}
    for name, (base, spread) in spreads.items():
        noise = np.random.default_rng([zlib.crc32(name.encode()), seed]).standard_normal(out[name].shape)
        drawn = base * np.exp(spread * noise) if base else spread * noise
        out[name] = jnp.asarray(drawn.astype(out[name].dtype))
    for name, factor in factors.items():
        out[name] = (out[name] * factor).astype(out[name].dtype)
    return out
```

```python
from contextlib import ExitStack

import numpy as np

import concourse.bass as bass
from concourse import mybir
from concourse.alu_op_type import AluOpType as ALU

F32 = mybir.dt.float32
F32R = mybir.dt.float32r
ACT = mybir.ActivationFunctionType
AX = mybir.AxisListType

P = 128
D = 1024
KT = D // P
DEPTH = 2
CTX_TILES, LAT_TILES = 2, 8
NT = CTX_TILES + LAT_TILES
NTOK = NT * P
HEADS, DK = 8, 64
PAIRS = HEADS // 2
CONV = 512
TAPS = 31
REACH = TAPS // 2
FF = 4 * D
IN_WIDTH = 6 * 512
GRID_W = 64
EPS = 1e-5
ALPHA = float((2 * DEPTH) ** 0.25)
K_SCALE = DK ** -0.5
UNIT = 1024
BLK = 256
NBLK = FF // BLK
RING = 6
IN_UNITS, OUT_UNITS = 24, 8
LAYER_UNITS = IN_UNITS + OUT_UNITS + 4 * NBLK
UT = REACH + CTX_TILES * P + 2 * REACH + LAT_TILES * P + REACH


def tiles_of(layer):
    return list(range(0 if layer < DEPTH - 1 else CTX_TILES, NT))


def chunks_of(layer):
    lat = [(CTX_TILES, 4), (CTX_TILES + 4, 4)]
    return ([(0, CTX_TILES)] if layer < DEPTH - 1 else []) + lat


GROUPS = [("AB", 0), ("Q", 0), ("Q", 1), ("AB", 1), ("Q", 2), ("Q", 3)]
TAPS_STEP = 3
ADA_BUFS = 4


def mix_in_plan(layer):
    tiles = tiles_of(layer)
    steps = []
    first_of = {}
    for kind, i in GROUPS:
        first_of[kind, i] = len(steps)
        steps += [(kind, i, t) for t in (tiles if kind == "AB" else range(NT))]
    group_of = [GROUPS.index((kind, i)) for kind, i, _ in steps]
    sizes = [group_of.count(g) for g in range(len(GROUPS))]
    starts = [group_of.index(g) for g in range(len(GROUPS))]
    plan, evacs, posts, ready = [], list(range(len(steps))), list(range(len(steps))), []
    scored, valued, scanned, evac_at, taps = set(), set(), set(), {}, []
    n = 0
    while n < len(steps) or posts or len(valued) < PAIRS * len(tiles):
        if n < len(steps):
            plan.append(("proj", n))
            g, j = group_of[n], n - starts[group_of[n]]
            if j in (2, 5):
                plan.append(("load", 4 * (g + 1) + (j == 5)))
            if j == sizes[g] - 1:
                plan += [("load", 4 * (g + 1) + 2), ("load", 4 * (g + 1) + 3)]
        if ready and ready[0] in scored:
            p, t = ready.pop(0)
            plan.append(("values", p, t))
            valued.add((p, t))
        if ready:
            plan.append(("scores", *ready[0]))
            scored.add(ready[0])
        while evacs and evacs[0] <= n:
            kind, p, t = steps[evacs[0]]
            if kind == "Q" and p and t in tiles and (p - 1, t) not in valued:
                break
            plan.append(("evac", evacs[0]))
            evac_at[evacs.pop(0)] = n
        k = 0
        while posts and k < 2 and evac_at.get(posts[0], n) < n:
            kind, p, t = steps[posts[0]]
            plan.append(("post", posts.pop(0)))
            k += 1
            if t == NT - 1:
                if kind == "Q":
                    plan.append(("scan", p))
                    assert not p or all((p - 1, u) in valued for u in tiles)
                    ready += [(p, u) for u in tiles]
                else:
                    taps += [(p, a, min(a + TAPS_STEP, 2 * TAPS)) for a in range(0, 2 * TAPS, TAPS_STEP)]
        if taps:
            plan.append(("taps", *taps.pop(0)))
        n += 1
    assert not taps
    return steps, plan


def shape_constants():
    f = np.float32
    i = np.arange(P, dtype=f)
    dist = i[None, :] - i[:, None]
    cols = np.stack([-(i + 1), -(P - i), -(P - 1 - i), -i], axis=1)
    inv = np.power(f(10000.0), -(np.arange(DK // 4, dtype=f) / f(DK // 4))).astype(f)
    n = np.arange(LAT_TILES * P)
    row, col = (n // GRID_W).astype(f), (n % GRID_W).astype(f)
    ang = np.concatenate([row[:, None] * inv, col[:, None] * inv], axis=-1).astype(f)
    cos, sin = np.cos(ang), np.sin(ang)
    one = np.ones((CTX_TILES * P, DK // 2), f)
    rope = np.stack([np.concatenate([one, cos]), np.concatenate([0 * one, sin])], axis=1)
    rope = rope.reshape(NT, P, 2, DK // 2).transpose(1, 0, 2, 3)
    const = np.concatenate([np.eye(P, dtype=f), -np.maximum(dist, 0), -np.maximum(-dist, 0), cols], axis=1)
    return {"const_cols": np.ascontiguousarray(const, dtype=f),
            "const_rope": np.ascontiguousarray(rope, dtype=f)}


def layer_counts(l):
    n = len(tiles_of(l))
    runs = len(chunks_of(l))
    conv_tiles, q_tiles, ret_steps = 2 * n, PAIRS * NT, PAIRS * n
    t_in, t_mlp = (1 + runs if l else runs) * KT, runs * KT
    hidden, shares = 2 * runs * NBLK, 2 * n * NBLK
    each = {
        1: "kdec_done mask_arg mask_exp one_added zero_set",
        2: "dec_op",
        n: "scaled cvt_done cnorm cn_var cn_pow conv_aff gn_cent gn_var gn_pow gn_norm mix_a mix_b mixtr_done "
           "mix_hi mix_lo silu_g sq_done ln_var ln_pow ln_shift ln_act ln_x ln1_done ln2_var ln2_pow ln2_shift "
           "ln2_act ln2_x ln2_done",
    }
    counts = {name: k for k, names in each.items() for name in names.split()}
    counts.update(
        x_in=0 if l else 32, small_in=160, conv_in=80, rope_in=32, rows_in=96, gate_in=64, gate2_in=64, cv_st=64,
        tr_in=t_in + t_mlp, hi_in=t_in + t_mlp, mod_in=t_in + t_mlp, split_in=t_in + t_mlp, gn_aff=2 * n,
        proj_done=conv_tiles + q_tiles, post_done=conv_tiles + q_tiles, post_evac=conv_tiles + q_tiles,
        sig_done=conv_tiles, glu_done=conv_tiles, conv_op=4 * TAPS * runs, scan_op=2 * NT * PAIRS,
        rot_part=4 * q_tiles, rot_done=2 * q_tiles,
        z_done=2 * n, z_read=2 * n, ctx_sum=0 if l == DEPTH - 1 else 2 * NBLK)
    for name in "qk_ready v_ready evac_q vdec_done u_done u_evac".split():
        counts[name] = q_tiles
    for name in "qd_done sd_done score_done prob_done val_done comb_a comb_b comb_done".split():
        counts[name] = ret_steps
    for name in "h_done relu_done h_sq h_high h_split".split():
        counts[name] = hidden
    for name in "y_done y_read y_add".split():
        counts[name] = shares
    pairs = {"g_st": 8 * q_tiles, "o_st": 8 * ret_steps}
    pairs.update({name: 8 * n for name in "o_in g_in cv_in res_in".split()})
    return counts, pairs


def build(nc, x, c, ctx, c_ctx, w_ada, b_ada, w_in, rate_f, rate_b, gn_w, gn_b, conv_w, conv_b,
          cln_w, cln_b, w_out, ln1_w, ln1_b, w_ff1, w_ff2, ln2_w, ln2_b, const_cols, const_rope, out):
    es = ExitStack()
    with es:
        es.enter_context(nc.allow_non_contiguous_dma(reason="small per-channel columns"))

        def sb(name, shape, dt=F32):
            return es.enter_context(nc.sbuf_tensor(name, shape, dt))

        def sem(name):
            return es.enter_context(nc.semaphore(name))

        ada_d = nc.dram_tensor("ada_rows", (DEPTH, 2, 6 * D), F32, kind="Internal").ap()
        o_d = nc.dram_tensor("retention_rows", (DEPTH, NTOK, 512), F32, kind="Internal").ap()
        g_d = nc.dram_tensor("gate_rows", (DEPTH, NTOK, 512), F32, kind="Internal").ap()
        cv_d = nc.dram_tensor("conv_columns", (DEPTH, 4, P, NTOK), F32, kind="Internal").ap()
        x_d = nc.dram_tensor("residual_rows", (LAT_TILES * P, D), F32, kind="Internal").ap()

        with nc.sbuf_tensor("plain_words", [P, 2, KT, NTOK], F32) as plain:
            """The same memory as x_hl, while float32 data that isn't split is in it."""
        x_hl = sb("x_hl", [P, 2, KT, NTOK], F32R)
        x_hi, x_lo = x_hl[:, 0], x_hl[:, 1]
        w_hi = sb("w_hi", [P, 4, UNIT], F32R)
        w_lo = sb("w_lo", [P, 4, UNIT], F32R)
        h_hi = sb("h_hi", [P, 2, NTOK], F32R)
        h_lo = sb("h_lo", [P, 2, NTOK], F32R)
        raw = sb("raw", [P, 2, UNIT])
        KEEP, Y_SIZE = 656, 6400
        WORK = KEEP + NT * D + Y_SIZE
        work = sb("work", [P, WORK])

        def carver(at, limit):
            state = [at]

            def take(*shape):
                n = int(np.prod(shape))
                piece = work[:, state[0]:state[0] + n]
                state[0] += n
                assert state[0] <= limit, (state[0], limit)
                if len(shape) == 2:
                    piece = piece.rearrange("p (a b) -> p a b", b=shape[1])
                elif len(shape) == 3:
                    piece = piece.rearrange("p (a b c) -> p a b c", b=shape[1], c=shape[2])
                return piece
            return take

        keep = carver(0, KEEP)
        ident = keep(P)
        expo = keep(4)
        neg_half = keep(16)
        decay = keep(2, HEADS)
        q_dec = keep(HEADS, 2)
        k_dec = keep(HEADS, 2)
        k_dec_raw = keep(HEADS, 2)
        c_dec = keep(2, PAIRS)
        cw = keep(4, TAPS)
        cb = keep(4)
        modc = keep(4, 2, KT)
        bn = keep(2, 12)
        mv = keep(2, 2)
        rs = keep(2, 1)
        shift = keep(2, 1)
        gstat = keep(2, 3 * HEADS)
        XA = KEEP
        YA = XA + NT * D
        X = work[:, XA:YA].rearrange("p (t d) -> p t d", d=D)

        m = carver(XA, WORK)
        v_sb = m(NT, P)
        qk_t = m(NT, 2, P)
        kv_u = m(NT, 2, DK)
        state = m(NT, 2, DK)
        u_t = m(2, UT)
        acc = m(NTOK)
        rope = m(NT, 2, DK // 2)
        masks = m(HEADS, P)
        qk_raw = m(2, 2 * P)
        qk_rot = m(2, 2 * P)
        rot_tmp = m(2 * P)
        v_dec = m(2 * P)
        g_out = m(2, P)
        probs = m(2, 2 * P)
        diag_both = m(8 * P)
        q_diag = diag_both[:, 0:4 * P].rearrange("p (a b) -> p a b", a=2)
        s_diag = diag_both[:, 4 * P:].rearrange("p (a b) -> p a b", a=2)
        inter = m(2 * P)
        o_out = m(2, P)
        sig = m(2 * P)
        u_sb = m(2, 2 * P)
        dist = inter.rearrange("p (a b) -> p a b", b=P)
        ident_s = o_out[:, 0, :]

        mod32 = carver(YA + 4096, WORK)(2, 512)
        y = carver(YA, WORK)
        rows = y(4, 512)
        gate_row = y(2, 512)
        g_in = y(2, 512)
        cv_in = y(2, 4, P)
        sq = y(512)
        z_t = y(512)
        ln1_rows = work[:, YA:YA + 2 * D].rearrange("p (a b) -> p a b", b=D)
        y = carver(YA, WORK)
        gate2 = y(2, D)
        relu = y(2, 512)
        act32 = y(2, 512)
        y_t = y(2, 512)
        ln2_rows = work[:, YA + 2 * D:YA + 4 * D].rearrange("p (a b) -> p a b", b=D)
        ada_w = [plain[:, i // 2, :, (i % 2) * 512:(i % 2) * 512 + 512] for i in range(ADA_BUFS)]
        y = carver(YA, WORK)
        cond = y(KT, 2)
        cond_s = y(KT, 2)
        ada_b = y(ADA_BUFS, 512)
        ada_o = y(2, 512)

        banks = [es.enter_context(nc.psum_tensor(f"bank{i}", [P, 512], F32)) for i in range(8)]
        ps_proj = banks[0:4]
        ps_tr, ps_u, ps_sc, ps_o = banks[4:8]

        raw_in = [sem(f"raw_in{i}") for i in range(2)]
        w_high, w_ready, w_used = sem("w_high"), sem("w_ready"), sem("w_used")
        const_in, half_set = sem("const_in"), sem("half_set")
        cond_in, cond_ready = sem("cond_in"), sem("cond_ready")
        adaw_in = [sem(f"adaw_in{i}") for i in range(ADA_BUFS)]
        ada_st = [sem(f"ada_st{i}") for i in range(2)]
        ada_done, ada_row = sem("ada_done"), sem("ada_row")
        dve_chain, out_st = sem("dve_chain"), sem("out_st")
        x_st = sem("x_st")

        counts, pairs = layer_counts(0)
        S = {name: sem(name) for name in counts}
        S.update({name: [sem(f"{name}{i}") for i in range(2)] for name in pairs})

        def counted_before(l):
            base = {name: 0 for name in S}
            for before in range(l):
                for part in layer_counts(before):
                    for name, count in part.items():
                        base[name] += count
            return base

        BEFORE = [counted_before(l) for l in range(DEPTH)]
        PLANS = [mix_in_plan(l) for l in range(DEPTH)]

        def unit_parts(l, u):
            if u < IN_UNITS:
                kind, i = GROUPS[u // 4]
                parts = []
                for kk in range(2):
                    k = 2 * (u % 4) + kk
                    w = w_in[l, k * P:(k + 1) * P, :]
                    if kind == "Q":
                        src = w[:, 0:4 * 512].rearrange("p (s c) -> p s c", s=4)[:, :, i * P:(i + 1) * P]
                    else:
                        src = w[:, 4 * 512:].rearrange("p (s c) -> p s c", s=2)[:, :, i * 2 * P:(i + 1) * 2 * P]
                    parts.append((slice(kk * 512, kk * 512 + 512), src))
                return parts
            u -= IN_UNITS
            if u < OUT_UNITS:
                k = 2 * (u % 4)
                src = w_out[l, k * P:(k + 2) * P, (u // 4) * 512:(u // 4 + 1) * 512]
                return [(slice(0, UNIT), src.rearrange("(k p) n -> p k n", p=P))]
            u -= OUT_UNITS
            return mlp_unit_parts(l, u // 4, u % 4)

        def mlp_unit_parts(l, b, s):
            if s < 2:
                src = w_ff1[l, :, bass.ds(b * BLK + s * P, P)].rearrange("(k p) n -> p k n", p=P)
            else:
                src = w_ff2[l, bass.ds(b * BLK + (s - 2) * P, P), :]
            return [(slice(0, UNIT), src)]

        def fetch(act, parity, parts):
            for cols, src in parts:
                dst = raw[:, parity, cols]
                if len(src.shape) == 3:
                    dst = dst.rearrange("p (a b) -> p a b", b=src.shape[2])
                act.dma_start(dst, src).then_inc(raw_in[parity], 32 // len(parts))

        def slot(s, part):
            if s < 4:
                return (w_hi, w_lo)[part][:, s, :]
            return (h_hi, h_lo)[part][:, :, :].rearrange("p a b -> p (a b)")[:, (s - 4) * UNIT:(s - 3) * UNIT]

        def slot_of(u):
            return u % RING if u < IN_UNITS + OUT_UNITS else (u - IN_UNITS - OUT_UNITS) % 4

        def unit_released(eng, l, u):
            s0, g = BEFORE[l], u // 4
            if u % 4 < 3:
                eng.wait_ge(w_used, (3 * 8 * l) + 3 * g + u % 4 + 1)
            elif u < IN_UNITS:
                eng.wait_ge(S["proj_done"], s0["proj_done"] + 1 + max(n for n, st in enumerate(PLANS[l][0]) if GROUPS.index(st[:2]) == g))
            else:
                eng.wait_ge(S["z_done"], s0["z_done"] + (g - 5) * len(tiles_of(l)))

        def slot_free(eng, l, u):
            n_in = IN_UNITS + OUT_UNITS
            if u < RING:
                if l:
                    n, nc_ = len(tiles_of(l - 1)), len(chunks_of(l - 1))
                    if u < 2:
                        eng.wait_ge(S["h_done"], BEFORE[l - 1]["h_done"] + 2 * nc_ * NBLK)
                    else:
                        eng.wait_ge(S["y_done"], BEFORE[l - 1]["y_done"] + 2 * n * NBLK)
            elif u < n_in:
                unit_released(eng, l, u - RING)
            else:
                unit_released(eng, l, {0: n_in - 2, 1: n_in - 1, 2: n_in - 6, 3: n_in - 5}[u - n_in])

        def split_high(act, l, u, following):
            un = l * LAYER_UNITS + u
            act.wait_ge(raw_in[un % 2], 32 * (un // 2 + 1))
            slot_free(act, l, u)
            nc.scalar.activation(slot(slot_of(u), 0), raw[:, un % 2, :], ACT.Copy).then_inc(w_high, 1)
            if following is not None:
                act.wait_ge(w_ready, un) if un else None
                fetch(act, (un + 1) % 2, unit_parts(*following))

        def next_unit(l, u):
            if u + 1 < LAYER_UNITS:
                return (l, u + 1)
            return (l + 1, 0) if l + 1 < DEPTH else None

        def split_low(pool, l, u):
            un = l * LAYER_UNITS + u
            pool.wait_ge(w_high, un + 1)
            s = slot_of(u)
            nc.gpsimd.tensor_tensor(slot(s, 1), raw[:, un % 2, :], slot(s, 0).bitcast(F32), ALU.subtract).then_inc(w_ready, 1)

        def three_passes(out_ps, hi, lo, whi, wlo, first, last):
            nc.tensor.matmul(out_ps, hi, whi, start=first, stop=False)
            nc.tensor.matmul(out_ps, hi, wlo, start=False, stop=False)
            return nc.tensor.matmul(out_ps, lo, whi, start=False, stop=last)

        def project(pe, l, u0, t, out_ps, first_tile, last_tile, done):
            cols = slice(t * P, (t + 1) * P)
            for k in range(KT):
                u = u0 + k // 2
                if first_tile and k % 2 == 0:
                    pe.wait_ge(w_ready, l * LAYER_UNITS + u + 1)
                wc = slice((k % 2) * 512, (k % 2) * 512 + 512)
                s = slot_of(u)
                mm = three_passes(out_ps, x_hi[:, k, cols], x_lo[:, k, cols], slot(s, 0)[:, wc], slot(s, 1)[:, wc],
                                  k == 0, k == KT - 1)
                if last_tile and k in (1, 3, 5):
                    mm.then_inc(w_used, 1)
            mm.then_inc(done, 1)

        def in_chunks(l, which):
            chunks = [(0, CTX_TILES)] + chunks_of(DEPTH - 1) if which == 0 else chunks_of(l)
            return [(t0, n, k) for t0, n in chunks for k in range(KT)]

        N_IN0 = len(in_chunks(0, 0))

        def cond_of(t):
            return 1 if t < CTX_TILES else 0

        def ln_source_ready(eng, l, which, t_last):
            if which:
                eng.wait_ge(S["ln1_done"], BEFORE[l]["ln1_done"] + tiles_of(l).index(t_last) + 1)
            elif l:
                eng.wait_ge(S["ln2_done"], BEFORE[l - 1]["ln2_done"] + tiles_of(l - 1).index(t_last) + 1)
            else:
                eng.wait_ge(S["x_in"], BEFORE[0]["x_in"] + 32)

        def conv_ranges(l):
            lat = 2 * REACH + CTX_TILES * P
            runs = [(CTX_TILES * P, 512, lat), (CTX_TILES * P + 512, 512, lat + 512)]
            return ([(0, CTX_TILES * P, 0)] if l < DEPTH - 1 else []) + runs

        def row_of(l, p, t):
            T = tiles_of(l)
            return p * len(T) + T.index(t)

        block = es.enter_context(nc.Block())

        @block.sync
        def _(sp):
            sp.dma_start(ident, const_cols[:, 0:P]).then_inc(const_in, 16)
            sp.dma_start(expo, const_cols[:, 3 * P:3 * P + 4]).then_inc(const_in, 16)
            sp.dma_start(cond[:, :, 0], c.rearrange("a (k p) -> p (a k)", p=P)).then_inc(cond_in, 16)
            sp.dma_start(cond[:, :, 1], c_ctx.rearrange("(k p) -> p k", p=P)).then_inc(cond_in, 16)
            NG = DEPTH * 12

            def ada_store(gi):
                sp.wait_ge(ada_row, gi + 1)
                l, j = gi // 12, gi % 12
                sp.dma_start(ada_d[l, :, j * 512:(j + 1) * 512], ada_o[0:2, gi % 2, :]).then_inc(ada_st[gi % 2], 16)

            def small_loads(l):
                for d, rate in enumerate((rate_f, rate_b)):
                    sp.dma_start(decay[:, d, :], rate[l].partition_broadcast(P)).then_inc(S["small_in"], 16)
                for i, sec in enumerate((0, 1, 3, 4)):
                    for cd in range(2):
                        sp.dma_start(modc[:, i, cd, :], ada_d[l, cd, sec * D:(sec + 1) * D].rearrange("(k p) -> p k", p=P)).then_inc(S["small_in"], 16)
                sp.dma_start(cb, conv_b[l].rearrange("(k p) -> p k", p=P)).then_inc(S["conv_in"], 16)
                for ct in range(4):
                    sp.dma_start(cw[:, ct, :], conv_w[l, :, ct * P:(ct + 1) * P].rearrange("w p -> p w")).then_inc(S["conv_in"], 16)

            for gi in range(NG):
                l, j, buf = gi // 12, gi % 12, gi % ADA_BUFS
                if gi >= ADA_BUFS:
                    sp.wait_ge(ada_row, gi - ADA_BUFS + 1)
                sp.dma_start(ada_w[buf], w_ada[l, :, j * 512:(j + 1) * 512].rearrange("(k p) n -> p k n", p=P)).then_inc(adaw_in[buf], 16)
                sp.dma_start(ada_b[0:2, buf, :], b_ada[l, j * 512:(j + 1) * 512].partition_broadcast(2)).then_inc(adaw_in[buf], 16)
                if gi == ADA_BUFS:
                    sp.dma_start(X[:, 0:CTX_TILES, :], ctx.rearrange("a (t p) d -> p (a t) d", p=P)).then_inc(S["x_in"], 16)
                    sp.dma_start(X[:, CTX_TILES:, :], x.rearrange("a (t p) d -> p (a t) d", p=P)).then_inc(S["x_in"], 16)
                if gi >= ADA_BUFS:
                    ada_store(gi - ADA_BUFS)
            for gi in range(NG - ADA_BUFS, NG - 2):
                ada_store(gi)
            ada_store(NG - 2)
            ada_store(NG - 1)
            for par in range(2):
                sp.wait_ge(ada_st[par], 16 * (NG // 2))

            for l in range(DEPTH):
                s0, T = BEFORE[l], tiles_of(l)
                n = len(T)
                if l == 0:
                    small_loads(l)
                else:
                    for i, (t0, nt) in enumerate(chunks_of(DEPTH - 1)):
                        ln_source_ready(sp, l, 0, t0 + nt - 1)
                        rows_at = slice((t0 - CTX_TILES) * P, (t0 - CTX_TILES + nt) * P)
                        sp.dma_start(x_d[rows_at, :].rearrange("(t p) d -> p t d", p=P), X[:, t0:t0 + nt, :]).then_inc(x_st, 16)
                sp.wait_ge(S["split_in"], s0["split_in"] + N_IN0)
                if l:
                    sp.wait_ge(x_st, 32)
                sp.dma_start(dist, const_cols[:, P:3 * P].rearrange("p (a b) -> p a b", b=P)).then_inc(S["rope_in"], 16)
                sp.dma_start(rope, const_rope).then_inc(S["rope_in"], 16)
                steps, plan = PLANS[l]
                q = 0
                R = len(conv_ranges(l))
                for a in plan:
                    if a[0] == "evac" and steps[a[1]][0] == "Q":
                        _, p, t = steps[a[1]]
                        sp.wait_ge(S["evac_q"], s0["evac_q"] + q + 1)
                        sp.dma_start(g_d[l, t * P:(t + 1) * P, p * P:(p + 1) * P], g_out[:, q % 2, :]).then_inc(S["g_st"][q % 2], 16)
                        q += 1
                    if a[0] == "values":
                        _, p, t = a
                        r = row_of(l, p, t)
                        sp.wait_ge(S["comb_done"], s0["comb_done"] + r + 1)
                        sp.dma_start(o_d[l, t * P:(t + 1) * P, p * P:(p + 1) * P], o_out[:, r % 2, :]).then_inc(S["o_st"][r % 2], 16)
                    if a[0] == "taps":
                        _, h, a0, a1 = a
                        for ct in range(2):
                            if a0 <= (ct + 1) * TAPS - 1 < a1:
                                sp.wait_ge(S["conv_op"], s0["conv_op"] + (h * 2 + ct + 1) * TAPS * R)
                                c0 = conv_ranges(l)[0][0]
                                sp.dma_start(cv_d[l, 2 * h + ct, :, c0:], acc[:, c0:]).then_inc(S["cv_st"], 16)
                for par in range(2):
                    sp.wait_ge(S["g_st"][par], s0["g_st"] + 16 * (NT * PAIRS // 2))
                    sp.wait_ge(S["o_st"][par], s0["o_st"] + 16 * (n * PAIRS // 2))
                sp.wait_ge(S["cv_st"], s0["cv_st"] + 64)
                for i, r in enumerate((gn_w, gn_b, cln_w, cln_b)):
                    sp.dma_start(rows[:, i, :], r[l].partition_broadcast(P)).then_inc(S["rows_in"], 16)
                for cd in range(2):
                    sp.dma_start(gate_row[:, cd, :], ada_d[l, cd, 2 * D:2 * D + 512].partition_broadcast(P)).then_inc(S["rows_in"], 16)

                def residual(j):
                    t = T[j]
                    sp.wait_ge(S["mixtr_done"], s0["mixtr_done"] + j + 1)
                    if j >= 2:
                        sp.wait_ge(S["z_read"], s0["z_read"] + j - 1)
                    if l:
                        src = x_d[(t - CTX_TILES) * P:(t - CTX_TILES + 1) * P, :]
                    elif t < CTX_TILES:
                        src = ctx[0, t * P:(t + 1) * P, :]
                    else:
                        src = x[0, (t - CTX_TILES) * P:(t - CTX_TILES + 1) * P, :]
                    sp.dma_start(X[:, t, :], src).then_inc(S["res_in"][j % 2], 16)

                for j in range(n):
                    t = T[j]
                    if j >= 2:
                        sp.wait_ge(S["mix_a"], s0["mix_a"] + j - 1)
                        sp.wait_ge(S["cvt_done"], s0["cvt_done"] + j - 1)
                    sp.dma_start(X[:, t, 0:512], o_d[l, t * P:(t + 1) * P, :]).then_inc(S["o_in"][j % 2], 16)
                    sp.dma_start(g_in[:, j % 2, :], g_d[l, t * P:(t + 1) * P, :]).then_inc(S["g_in"][j % 2], 16)
                    sp.dma_start(cv_in[:, j % 2, :, :], cv_d[l, :, :, t * P:(t + 1) * P].rearrange("c p n -> p c n")).then_inc(S["cv_in"][j % 2], 16)
                    if j >= 2:
                        residual(j - 2)
                residual(n - 2)
                residual(n - 1)
                for cd in range(2):
                    sp.dma_start(g_in[:, cd, :], ada_d[l, cd, 2 * D + 512:3 * D].partition_broadcast(P)).then_inc(S["gate_in"], 16)
                for i, r in enumerate((ln1_w, ln1_b)):
                    sp.dma_start(ln1_rows[:, i, :], r[l].partition_broadcast(P)).then_inc(S["gate_in"], 16)
                sp.wait_ge(S["ln1_done"], s0["ln1_done"] + n)
                sp.wait_ge(S["split_in"], s0["split_in"] + N_IN0 + len(in_chunks(l, 1)))
                for cd in range(2):
                    sp.dma_start(gate2[:, cd, :], ada_d[l, cd, 5 * D:6 * D].partition_broadcast(P)).then_inc(S["gate2_in"], 16)
                sp.wait_ge(S["h_split"], s0["h_split"] + 2 * len(chunks_of(l)) * NBLK)
                for i, r in enumerate((ln2_w, ln2_b)):
                    sp.dma_start(ln2_rows[:, i, :], r[l].partition_broadcast(P)).then_inc(S["gate2_in"], 16)
                if l + 1 < DEPTH:
                    small_loads(l + 1)
                if l == DEPTH - 1:
                    for j, t in enumerate(T):
                        sp.wait_ge(S["ln2_done"], s0["ln2_done"] + j + 1)
                        sp.dma_start(out[0, (t - CTX_TILES) * P:(t - CTX_TILES + 1) * P, :], X[:, t, :]).then_inc(out_st, 16)
            sp.wait_ge(out_st, 16 * LAT_TILES)

        @block.tensor
        def _(pe):
            pe.wait_ge(cond_ready, 1)
            for gi in range(DEPTH * 12):
                pe.wait_ge(adaw_in[gi % ADA_BUFS], 32 * (gi // ADA_BUFS + 1))
                if gi >= 2:
                    pe.wait_ge(ada_row, gi - 1)
                for k in range(KT):
                    mm = nc.tensor.matmul(banks[6 + gi % 2][0:2, :], cond_s[:, k, :], ada_w[gi % ADA_BUFS][:, k, :], start=k == 0, stop=k == KT - 1)
                mm.then_inc(ada_done, 1)

            def transpose_in(l, which):
                s0, base = BEFORE[l], N_IN0 * which
                for j, (t0, n, k) in enumerate(in_chunks(l, which)):
                    if k == 0:
                        ln_source_ready(pe, l, which, t0 + n - 1)
                    if j >= 2:
                        pe.wait_ge(S["mod_in"], s0["mod_in"] + base + j - 1)
                    for i in range(n):
                        mm = nc.tensor.transpose(banks[j % 2][:, i * P:(i + 1) * P], X[:, t0 + i, k * P:(k + 1) * P], ident)
                    mm.then_inc(S["tr_in"], 1)

            for l in range(DEPTH):
                s0, T = BEFORE[l], tiles_of(l)
                n = len(T)
                transpose_in(l, 0)
                pe.wait_ge(S["split_in"], s0["split_in"] + N_IN0)
                pe.wait_ge(S["zero_set"], s0["zero_set"] + 1)
                steps, plan = PLANS[l]
                qn = [sum(st[0] == "Q" for st in steps[:i]) for i in range(len(steps) + 1)]
                for a in plan:
                    if a[0] == "proj":
                        i = a[1]
                        kind, p, t = steps[i]
                        g = GROUPS.index((kind, p))
                        if i >= 4:
                            if steps[i - 4][0] == "Q":
                                pe.wait_ge(S["evac_q"], s0["evac_q"] + qn[i - 3])
                            else:
                                pe.wait_ge(S["glu_done"], s0["glu_done"] + i - 3 - qn[i - 3])
                        project(pe, l, 4 * g, t, ps_proj[i % 4][:, :], i == 0 or steps[i - 1][:2] != steps[i][:2],
                                i + 1 == len(steps) or steps[i + 1][:2] != steps[i][:2], S["proj_done"])
                    elif a[0] == "post":
                        i = a[1]
                        kind, p, t = steps[i]
                        if i:
                            pe.wait_ge(S["post_evac"], s0["post_evac"] + i)
                        if kind == "AB":
                            pe.wait_ge(S["glu_done"], s0["glu_done"] + i - qn[i] + 1)
                            src = u_sb[:, (i - qn[i]) % 2, :]
                        else:
                            pe.wait_ge(S["rot_done"], s0["rot_done"] + 2 * (qn[i] + 1))
                            src = qk_rot[:, qn[i] % 2, :]
                        for h in range(2):
                            mm = nc.tensor.transpose(ps_tr[:, h * P:(h + 1) * P], src[:, h * P:(h + 1) * P], ident)
                        mm.then_inc(S["post_done"], 1)
                        if kind == "Q":
                            pe.wait_ge(S["vdec_done"], s0["vdec_done"] + qn[i] + 1)
                            if qn[i]:
                                pe.wait_ge(S["u_evac"], s0["u_evac"] + qn[i])
                            nc.tensor.matmul(ps_u[:, 0:2 * P], src[:, P:2 * P], v_dec, start=True, stop=True).then_inc(S["u_done"], 1)
                    elif a[0] == "scores":
                        _, p, t = a
                        r = row_of(l, p, t)
                        pe.wait_ge(S["qd_done"], s0["qd_done"] + r + 1)
                        if r:
                            pe.wait_ge(S["prob_done"], s0["prob_done"] + r)
                        nc.tensor.matmul(ps_sc[:, 0:2 * P], qk_t[:, t, 1, :], q_diag[:, r % 2, :], start=True, stop=True).then_inc(S["score_done"], 1)
                    elif a[0] == "values":
                        _, p, t = a
                        r = row_of(l, p, t)
                        pe.wait_ge(S["prob_done"], s0["prob_done"] + r + 1)
                        pe.wait_ge(S["sd_done"], s0["sd_done"] + r + 1)
                        if r:
                            pe.wait_ge(S["comb_b"], s0["comb_b"] + r)
                        for h in range(2):
                            nc.tensor.matmul(ps_o[:, h * DK:(h + 1) * DK], probs[:, r % 2, h * P:(h + 1) * P], v_sb[:, t, h * DK:(h + 1) * DK], start=True, stop=True)
                        nc.tensor.matmul(ps_o[:, P:3 * P], qk_t[:, t, 0, :], s_diag[:, r % 2, :], start=True, stop=True).then_inc(S["val_done"], 1)
                ps_c, ps_z, ps_m = banks[4:6], banks[2:4], banks[0:2]
                for st in range(n + 2):
                    if st < n:
                        pe.wait_ge(S["cv_in"][st % 2], s0["cv_in"] + 16 * (st // 2 + 1))
                        if st >= 2:
                            pe.wait_ge(S["cnorm"], s0["cnorm"] + st - 1)
                        elif st == 0:
                            pe.wait_ge(S["post_evac"], s0["post_evac"] + len(steps))
                            pe.wait_ge(S["u_evac"], s0["u_evac"] + NT * PAIRS)
                        for ct in range(4):
                            mm = nc.tensor.transpose(ps_c[st % 2][:, ct * P:(ct + 1) * P], cv_in[:, st % 2, ct, :], ident)
                        mm.then_inc(S["cvt_done"], 1)
                    j = st - 1
                    if 0 <= j < n:
                        pe.wait_ge(S["mix_a"], s0["mix_a"] + j + 1)
                        pe.wait_ge(S["mix_b"], s0["mix_b"] + j + 1)
                        if j:
                            pe.wait_ge(S["mix_lo"], s0["mix_lo"] + j)
                        for k in range(KT):
                            mm = nc.tensor.transpose(ps_m[k // 4][:, (k % 4) * P:(k % 4 + 1) * P], X[:, T[j], k * P:(k + 1) * P], ident)
                        mm.then_inc(S["mixtr_done"], 1)
                    j = st - 2
                    if j >= 0:
                        pe.wait_ge(S["mix_lo"], s0["mix_lo"] + j + 1)
                        if j >= 2:
                            pe.wait_ge(S["z_read"], s0["z_read"] + j - 1)
                        project(pe, l, IN_UNITS, T[j], ps_z[j % 2][:, :], j == 0, j == n - 1, S["z_done"])
                for j in range(n):
                    pe.wait_ge(S["z_read"], s0["z_read"] + n + j - 1)
                    project(pe, l, IN_UNITS + 4, T[j], ps_z[j % 2][:, :], j == 0, j == n - 1, S["z_done"])
                transpose_in(l, 1)
                pe.wait_ge(S["split_in"], s0["split_in"] + N_IN0 + len(in_chunks(l, 1)))
                chunks = chunks_of(l)
                HB, YB = 2 * len(chunks), 2 * n
                u0 = l * LAYER_UNITS + IN_UNITS + OUT_UNITS

                def mlp_block(b, first):
                    for ci, (t0, nt) in enumerate(chunks):
                        for f in range(2):
                            j = 2 * ci + f
                            if ci == 0:
                                pe.wait_ge(w_ready, b * 4 + (u0 + f + 1))
                            if j >= 2 or not first:
                                pe.wait_ge(S["relu_done"], s0["relu_done"] + b * HB + (j - 1))
                            if l < DEPTH - 1 and j in (2, 3):
                                pe.wait_ge(S["ctx_sum"], s0["ctx_sum"] + b * 2 + (j - 1))
                            cols = slice(t0 * P, (t0 + nt) * P)
                            if nt == CTX_TILES:
                                both = banks[j % 2][:, :].rearrange("p (a n) -> p a n", a=2)
                                for k in range(KT):
                                    wc = slice(k * P, (k + 1) * P)
                                    nc.tensor.matmul(both, slot(f, 0)[:, wc], x_hl[:, :, k, cols], start=k == 0, stop=False)
                                    mm = nc.tensor.matmul(both[:, 0, :], slot(f, 1)[:, wc], x_hi[:, k, cols], start=False, stop=k == KT - 1)
                                mm.then_inc(S["h_done"], 1)
                                continue
                            for k in range(KT):
                                wc = slice(k * P, (k + 1) * P)
                                o = banks[j % 2][:, 0:nt * P]
                                nc.tensor.matmul(o, slot(f, 0)[:, wc], x_hi[:, k, cols], start=k == 0, stop=False)
                                nc.tensor.matmul(o, slot(f, 0)[:, wc], x_lo[:, k, cols], start=False, stop=False)
                                mm = nc.tensor.matmul(o, slot(f, 1)[:, wc], x_hi[:, k, cols], start=False, stop=k == KT - 1)
                            mm.then_inc(S["h_done"], 1)
                    for ti, t in enumerate(T):
                        for half in range(2):
                            yi = 2 * ti + half
                            if yi == 0:
                                pe.wait_ge(w_ready, b * 4 + (u0 + 4))
                            for ci, (t0, _) in enumerate(chunks):
                                if t == t0 and half == 0:
                                    pe.wait_ge(S["h_split"], s0["h_split"] + b * HB + 2 * (ci + 1))
                            if yi >= 4 or not first:
                                pe.wait_ge(S["y_read"], s0["y_read"] + b * YB + (yi - 3))
                            for f in range(2):
                                wc = slice(half * 512, (half + 1) * 512)
                                cols = slice(t * P, (t + 1) * P)
                                mm = three_passes(banks[2 + yi % 4][:, :], h_hi[:, f, cols], h_lo[:, f, cols],
                                                  slot(2 + f, 0)[:, wc], slot(2 + f, 1)[:, wc], f == 0, f == 1)
                            mm.then_inc(S["y_done"], 1)

                mlp_block(0, True)
                with pe.Fori(1, NBLK) as b:
                    mlp_block(b, False)

        @block.scalar
        def _(act):
            act.wait_ge(cond_in, 32)
            nc.scalar.activation(cond_s, cond, ACT.Silu).then_inc(cond_ready, 1)
            fetch(act, 0, unit_parts(0, 0))

            def layer_norm_part(l, ln):
                for j, t in enumerate(tiles_of(l)):
                    act.wait_ge(S[ln + "_shift"], BEFORE[l][ln + "_shift"] + j + 1)
                    nc.scalar.activation(X[:, t, :], X[:, t, :], ACT.Identity, bias=shift[:, j % 2, :], scale=rs[:, j % 2, :]).then_inc(S[ln + "_act"], 1)

            def load(l, u):
                split_high(act, l, u, next_unit(l, u))

            def transpose_in(l, which):
                s0, base = BEFORE[l], N_IN0 * which
                for j, (t0, n, k) in enumerate(in_chunks(l, which)):
                    if which and j in (4, 10):
                        load(l, IN_UNITS + OUT_UNITS + (2 if j == 4 else 3))
                    act.wait_ge(S["tr_in"], s0["tr_in"] + base + j + 1)
                    if j >= 2:
                        act.wait_ge(S["split_in"], s0["split_in"] + base + j - 1)
                    cd = cond_of(t0)
                    nc.scalar.activation(mod32[:, j % 2, 0:n * P], banks[j % 2][:, 0:n * P], ACT.Identity,
                                         bias=modc[:, 2 * which, cd, k:k + 1], scale=modc[:, 2 * which + 1, cd, k:k + 1]).then_inc(S["mod_in"], 1)

            for l in range(DEPTH):
                s0, T = BEFORE[l], tiles_of(l)
                n = len(T)
                for u in range(0 if l == 0 else 2, 4):
                    load(l, u)
                act.wait_ge(S["one_added"], s0["one_added"] + 1)
                transpose_in(l, 0)
                act.wait_ge(S["small_in"], s0["small_in"] + 160)
                nc.scalar.activation(decay, decay, ACT.Exp).then_inc(S["dec_op"], 1)
                act.wait_ge(S["dec_op"], s0["dec_op"] + 1)
                act.wait_ge(const_in, 32)
                nc.scalar.activation(q_dec[:, :, 0], decay[:, 0, :], ACT.Exp, scale=expo[:, 0:1])
                nc.scalar.activation(q_dec[:, :, 1], decay[:, 1, :], ACT.Exp, scale=expo[:, 1:2])
                nc.scalar.activation(k_dec_raw[:, :, 0], decay[:, 0, :], ACT.Exp, scale=expo[:, 2:3])
                nc.scalar.activation(k_dec_raw[:, :, 1], decay[:, 1, :], ACT.Exp, scale=expo[:, 3:4])
                for h in range(2):
                    rows64 = slice(h * DK, (h + 1) * DK)
                    last = nc.scalar.activation(c_dec[rows64, :, :], decay[rows64, :, h::2], ACT.Exp, scale=-float(P))
                last.then_inc(S["dec_op"], 1)
                act.wait_ge(S["mask_arg"], s0["mask_arg"] + 1)
                nc.scalar.activation(masks, masks, ACT.Exp).then_inc(S["mask_exp"], 1)
                if l:
                    act.wait_ge(x_st, 32)
                act.wait_ge(S["split_in"], s0["split_in"] + N_IN0)
                steps, plan = PLANS[l]
                qn = [sum(st[0] == "Q" for st in steps[:i]) for i in range(len(steps) + 1)]
                R = len(conv_ranges(l))
                act.wait_ge(S["zero_set"], s0["zero_set"] + 1)
                for a in plan:
                    if a[0] == "load":
                        load(l, a[1])
                    elif a[0] == "evac":
                        i = a[1]
                        kind, p, t = steps[i]
                        ps = ps_proj[i % 4]
                        act.wait_ge(S["proj_done"], s0["proj_done"] + i + 1)
                        if kind == "AB":
                            ab = i - qn[i]
                            if ab:
                                act.wait_ge(S["glu_done"], s0["glu_done"] + ab)
                            nc.scalar.activation(sig, ps[:, 2 * P:4 * P], ACT.Sigmoid).then_inc(S["sig_done"], 1)
                        else:
                            q = qn[i]
                            if q >= 2:
                                act.wait_ge(S["rot_done"], s0["rot_done"] + 2 * (q - 1))
                            nc.scalar.activation(qk_raw[:, q % 2, :], ps[:, 0:2 * P], ACT.Copy).then_inc(S["qk_ready"], 1)
                            if p:
                                act.wait_ge(S["vdec_done"], s0["vdec_done"] + q - NT + 1)
                                if t in T:
                                    act.wait_ge(S["val_done"], s0["val_done"] + row_of(l, p - 1, t) + 1)
                            nc.scalar.activation(v_sb[:, t, :], ps[:, 2 * P:3 * P], ACT.Copy).then_inc(S["v_ready"], 1)
                            if q >= 2:
                                act.wait_ge(S["g_st"][q % 2], s0["g_st"] + 16 * (q // 2))
                            nc.scalar.activation(g_out[:, q % 2, :], ps[:, 3 * P:4 * P], ACT.Copy).then_inc(S["evac_q"], 1)
                    elif a[0] == "post":
                        i = a[1]
                        kind, p, t = steps[i]
                        act.wait_ge(S["post_done"], s0["post_done"] + i + 1)
                        if kind == "AB":
                            if p:
                                act.wait_ge(S["conv_op"], s0["conv_op"] + 2 * TAPS * R)
                            at = REACH + t * P + (2 * REACH if t >= CTX_TILES else 0)
                            nc.scalar.activation(u_t[:, :, at:at + P], ps_tr[:, 0:2 * P].rearrange("p (a b) -> p a b", b=P), ACT.Copy).then_inc(S["post_evac"], 1)
                        else:
                            nc.scalar.activation(qk_t[:, t, :, :], ps_tr[:, 0:2 * P].rearrange("p (a b) -> p a b", b=P), ACT.Copy).then_inc(S["post_evac"], 1)
                            act.wait_ge(S["u_done"], s0["u_done"] + qn[i] + 1)
                            if p:
                                act.wait_ge(S["scan_op"], s0["scan_op"] + 2 * NT * p)
                            for h in range(2):
                                r64 = slice(h * DK, (h + 1) * DK)
                                last = nc.scalar.activation(kv_u[r64, t, :, :], ps_u[r64, h * P:(h + 1) * P].rearrange("p (a b) -> p a b", b=DK), ACT.Copy)
                            last.then_inc(S["u_evac"], 1)
                    elif a[0] == "scores":
                        _, p, t = a
                        r = row_of(l, p, t)
                        if r >= 2:
                            act.wait_ge(S["score_done"], s0["score_done"] + r - 1)
                        act.wait_ge(S["post_evac"], s0["post_evac"] + 1 + steps.index(("Q", p, t)))
                        for h in range(2):
                            r64 = slice(h * DK, (h + 1) * DK)
                            last = nc.scalar.activation(q_diag[r64, r % 2, h * P:(h + 1) * P], qk_t[r64, t, 0, :], ACT.Copy)
                        last.then_inc(S["qd_done"], 1)
                    elif a[0] == "values":
                        _, p, t = a
                        r = row_of(l, p, t)
                        act.wait_ge(S["scan_op"], s0["scan_op"] + 2 * NT * (p + 1))
                        if r >= 2:
                            act.wait_ge(S["val_done"], s0["val_done"] + r - 1)
                        for h in range(2):
                            r64 = slice(h * DK, (h + 1) * DK)
                            last = nc.scalar.activation(s_diag[r64, r % 2, h * P:(h + 1) * P].rearrange("p (a b) -> p a b", b=DK), state[r64, t, :, :], ACT.Copy)
                        last.then_inc(S["sd_done"], 1)
                for st in range(n + 2):
                    if st < n:
                        act.wait_ge(S["g_in"][st % 2], s0["g_in"] + 16 * (st // 2 + 1))
                        nc.scalar.activation(g_in[:, st % 2, :], g_in[:, st % 2, :], ACT.Silu).then_inc(S["silu_g"], 1)
                        act.wait_ge(S["gn_cent"], s0["gn_cent"] + st + 1)
                        if st:
                            act.wait_ge(S["gn_var"], s0["gn_var"] + st)
                        nc.scalar.activation(sq, X[:, T[st], 0:512], ACT.Square).then_inc(S["sq_done"], 1)
                    j = st - 1
                    if 0 <= j < n:
                        act.wait_ge(S["mixtr_done"], s0["mixtr_done"] + j + 1)
                        for half in range(2):
                            dst = x_hi[:, 4 * half:4 * half + 4, T[j] * P:(T[j] + 1) * P]
                            last = nc.scalar.activation(dst, banks[half][:, :].rearrange("p (a b) -> p a b", b=P), ACT.Copy)
                        last.then_inc(S["mix_hi"], 1)
                    if st < n:
                        act.wait_ge(S["conv_aff"], s0["conv_aff"] + st + 1)
                        nc.scalar.activation(X[:, T[st], 512:D], X[:, T[st], 512:D], ACT.Silu).then_inc(S["mix_b"], 1)
                    if st in (1, 2):
                        load(l, IN_UNITS + 3 + st)
                load(l, IN_UNITS + 6)
                load(l, IN_UNITS + 7)
                layer_norm_part(l, "ln")
                load(l, IN_UNITS + OUT_UNITS)
                load(l, IN_UNITS + OUT_UNITS + 1)
                transpose_in(l, 1)
                act.wait_ge(S["tr_in"], s0["tr_in"] + N_IN0 + len(in_chunks(l, 1)))
                for t in T:
                    nc.scalar.activation(X[:, t, :], X[:, t, :], ACT.Copy, scale=ALPHA).then_inc(S["scaled"], 1)
                act.wait_ge(S["gate2_in"], s0["gate2_in"] + 32)
                chunks = chunks_of(l)
                HB, YB = 2 * len(chunks), 2 * n
                u0 = l * LAYER_UNITS + IN_UNITS + OUT_UNITS

                def mlp_block(b, next_fetches, first=False):
                    for j in range(HB):
                        nt = chunks[j // 2][1]
                        act.wait_ge(S["h_done"], s0["h_done"] + b * HB + (j + 1))
                        if j >= 2 or not first:
                            act.wait_ge(S["h_sq"], s0["h_sq"] + b * HB + (j - 1))
                        if nt == CTX_TILES:
                            nc.scalar.activation(relu[:, j % 2, 0:nt * P], banks[j % 2][:, nt * P:2 * nt * P], ACT.Copy).then_inc(S["relu_done"], 1)
                        else:
                            nc.scalar.activation(relu[:, j % 2, 0:nt * P], banks[j % 2][:, 0:nt * P], ACT.Relu).then_inc(S["relu_done"], 1)
                    for sl, following in enumerate(next_fetches):
                        if sl == 2:
                            act.wait_ge(S["y_done"], s0["y_done"] + b * YB + YB)
                        un = u0 + 4 + sl
                        act.wait_ge(raw_in[un % 2], b * 64 + 32 * (un // 2 + 1))
                        nc.scalar.activation(slot(sl, 0), raw[:, un % 2, :], ACT.Copy).then_inc(w_high, 1)
                        if following is not None:
                            act.wait_ge(w_ready, b * 4 + un)
                            fetch(act, (un + 1) % 2, following)

                mlp_block(0, [mlp_unit_parts(l, 1, 1), mlp_unit_parts(l, 1, 2), mlp_unit_parts(l, 1, 3),
                              mlp_unit_parts(l, 2, 0)], first=True)
                with act.Fori(1, NBLK - 2) as b:
                    mlp_block(b, [mlp_unit_parts(l, b + 1, 1), mlp_unit_parts(l, b + 1, 2),
                                        mlp_unit_parts(l, b + 1, 3), mlp_unit_parts(l, b + 2, 0)])
                more = l + 1 < DEPTH
                mlp_block(NBLK - 2, [mlp_unit_parts(l, NBLK - 1, 1), mlp_unit_parts(l, NBLK - 1, 2),
                                           mlp_unit_parts(l, NBLK - 1, 3), unit_parts(l + 1, 0) if more else None])
                mlp_block(NBLK - 1, [unit_parts(l + 1, 1), unit_parts(l + 1, 2)] if more else [])
                layer_norm_part(l, "ln2")

        @block.gpsimd
        def _(pool):
            nc.gpsimd.memset(neg_half, -0.5).then_inc(half_set, 1)
            pool.wait_ge(half_set, 1)

            for l in range(DEPTH):
                s0, T = BEFORE[l], tiles_of(l)
                n = len(T)
                for u in range(0 if l == 0 else 2, 4):
                    split_low(pool, l, u)
                pool.wait_ge(S["split_in"], s0["split_in"] + N_IN0)
                if l:
                    pool.wait_ge(x_st, 32)
                nc.gpsimd.memset(diag_both, 0.0).then_inc(S["zero_set"], 1)
                steps, plan = PLANS[l]
                q = 0
                for a in plan:
                    if a[0] == "load":
                        split_low(pool, l, a[1])
                    elif a[0] == "evac" and steps[a[1]][0] == "Q":
                        _, p, t = steps[a[1]]
                        if q == 0:
                            pool.wait_ge(S["rope_in"], s0["rope_in"] + 32)
                            pool.wait_ge(S["kdec_done"], s0["kdec_done"] + 1)
                        pool.wait_ge(S["qk_ready"], s0["qk_ready"] + q + 1)
                        if q >= 2:
                            pool.wait_ge(S["u_done"], s0["u_done"] + q - 1)
                        src = qk_raw[:, q % 2, :].rearrange("p (h f e) -> p h f e", h=4, e=2)
                        dst = qk_rot[:, q % 2, :].rearrange("p (h f e) -> p h f e", h=4, e=2)
                        tmp = rot_tmp.rearrange("p (h f e) -> p h f e", h=4, e=2)
                        half = [P, 4, DK // 2]
                        cos = rope[:, t, 0, :].unsqueeze(1).to_broadcast(half)
                        sin = rope[:, t, 1, :].unsqueeze(1).to_broadcast(half)
                        if q:
                            pool.wait_ge(S["rot_done"], s0["rot_done"] + 2 * q)
                        for e in range(2):
                            nc.gpsimd.tensor_tensor(dst[:, :, :, e], src[:, :, :, e], cos, ALU.mult).then_inc(S["rot_part"], 1)
                            nc.gpsimd.tensor_tensor(tmp[:, :, :, e], src[:, :, :, 1 - e], sin, ALU.mult).then_inc(S["rot_part"], 1)
                        pool.wait_ge(S["rot_part"], s0["rot_part"] + 4 * (q + 1))
                        nc.gpsimd.tensor_tensor(dst[:, :, :, 0], dst[:, :, :, 0], tmp[:, :, :, 0], ALU.subtract).then_inc(S["rot_done"], 1)
                        nc.gpsimd.tensor_tensor(dst[:, :, :, 1], dst[:, :, :, 1], tmp[:, :, :, 1], ALU.add).then_inc(S["rot_done"], 1)
                        pool.wait_ge(S["v_ready"], s0["v_ready"] + q + 1)
                        if q:
                            pool.wait_ge(S["u_done"], s0["u_done"] + q)
                        kd = k_dec_raw if (l == DEPTH - 1 and t < CTX_TILES) else k_dec
                        by_head = [P, 2, 2, DK]
                        nc.gpsimd.tensor_tensor(v_dec.rearrange("p (h d e) -> p h d e", h=2, d=2),
                                                v_sb[:, t, :].rearrange("p (h e) -> p h e", h=2).unsqueeze(2).to_broadcast(by_head),
                                                kd[:, 2 * p:2 * p + 2, :].unsqueeze(3).to_broadcast(by_head), ALU.mult).then_inc(S["vdec_done"], 1)
                        q += 1
                pool.wait_ge(S["rows_in"], s0["rows_in"] + 96)
                for st in range(n + 1):
                    if st < n:
                        pool.wait_ge(S["cn_var"], s0["cn_var"] + st + 1)
                        nc.gpsimd.tensor_tensor(rs[:, st % 2, :], mv[:, st % 2, 1:2], neg_half[:, 0:1], ALU.pow).then_inc(S["cn_pow"], 1)
                        pool.wait_ge(S["gn_var"], s0["gn_var"] + st + 1)
                        nc.gpsimd.tensor_tensor(gstat[:, st % 2, 2 * HEADS:], gstat[:, st % 2, HEADS:2 * HEADS], neg_half[:, 0:HEADS], ALU.pow).then_inc(S["gn_pow"], 1)
                        o = X[:, T[st], 0:512]
                        pool.wait_ge(S["gn_norm"], s0["gn_norm"] + st + 1)
                        nc.gpsimd.tensor_tensor(o, o, rows[:, 0, :], ALU.mult).then_inc(S["gn_aff"], 1)
                        pool.wait_ge(S["gn_aff"], s0["gn_aff"] + 2 * st + 1)
                        nc.gpsimd.tensor_tensor(o, o, rows[:, 1, :], ALU.add).then_inc(S["gn_aff"], 1)
                        pool.wait_ge(S["gn_aff"], s0["gn_aff"] + 2 * st + 2)
                        pool.wait_ge(S["silu_g"], s0["silu_g"] + st + 1)
                        nc.gpsimd.tensor_tensor(o, o, g_in[:, st % 2, :], ALU.mult).then_inc(S["mix_a"], 1)
                    if st in (1, 2):
                        split_low(pool, l, IN_UNITS + 3 + st)
                for u in (6, 7):
                    split_low(pool, l, IN_UNITS + u)

                def layer_norm_part(ln, done, ln_rows):
                    for st in range(n + 2):
                        if st < n:
                            pool.wait_ge(S[ln + "_var"], s0[ln + "_var"] + st + 1)
                            if st >= 2:
                                pool.wait_ge(S[ln + "_act"], s0[ln + "_act"] + st - 1)
                            nc.gpsimd.tensor_tensor(rs[:, st % 2, :], mv[:, st % 2, 1:2], neg_half[:, 0:1], ALU.pow).then_inc(S[ln + "_pow"], 1)
                        if st >= 2:
                            pool.wait_ge(S[ln + "_x"], s0[ln + "_x"] + st - 1)
                            xt = X[:, T[st - 2], :]
                            nc.gpsimd.tensor_tensor(xt, xt, ln_rows[:, 1, :], ALU.add).then_inc(done, 1)

                pool.wait_ge(S["gate_in"], s0["gate_in"] + 64)
                layer_norm_part("ln", S["ln1_done"], ln1_rows)
                for u in range(4):
                    split_low(pool, l, IN_UNITS + OUT_UNITS + u)
                u0 = l * LAYER_UNITS + IN_UNITS + OUT_UNITS

                def mlp_block(b, units):
                    for sl in range(units):
                        un = u0 + 4 + sl
                        pool.wait_ge(w_high, b * 4 + (un + 1))
                        nc.gpsimd.tensor_tensor(slot(sl, 1), raw[:, un % 2, :], slot(sl, 0).bitcast(F32), ALU.subtract).then_inc(w_ready, 1)

                with pool.Fori(0, NBLK - 1) as b:
                    mlp_block(b, 4)
                mlp_block(NBLK - 1, 2 if l + 1 < DEPTH else 0)
                pool.wait_ge(S["gate2_in"], s0["gate2_in"] + 64)
                layer_norm_part("ln2", S["ln2_done"], ln2_rows)

        @block.vector
        def _(dve):
            chained = [0]

            def link(ins):
                chained[0] += 1
                ins.then_inc(dve_chain, 1)
                dve.wait_ge(dve_chain, chained[0])

            for gi in range(DEPTH * 12):
                dve.wait_ge(ada_done, gi + 1)
                if gi >= 2:
                    dve.wait_ge(ada_st[gi % 2], 16 * (gi // 2))
                nc.vector.tensor_tensor(ada_o[0:2, gi % 2, :], banks[6 + gi % 2][0:2, :], ada_b[0:2, gi % ADA_BUFS, :], ALU.add).then_inc(ada_row, 1)

            def transpose_in(l, which):
                s0, base = BEFORE[l], N_IN0 * which
                for j, (t0, n, k) in enumerate(in_chunks(l, which)):
                    cols = slice(t0 * P, (t0 + n) * P)
                    m32 = mod32[:, j % 2, 0:n * P]
                    dve.wait_ge(S["mod_in"], s0["mod_in"] + base + j + 1)
                    nc.vector.tensor_copy(x_hi[:, k, cols], m32).then_inc(S["hi_in"], 1)
                    dve.wait_ge(S["hi_in"], s0["hi_in"] + base + j + 1)
                    nc.vector.tensor_tensor(x_lo[:, k, cols], m32, x_hi[:, k, cols].bitcast(F32), ALU.subtract).then_inc(S["split_in"], 1)

            def row_stats(par, t, done):
                for half in range(2):
                    nc.vector.bn_stats(bn[:, par, 6 * half:6 * half + 6], X[:, t, half * 512:(half + 1) * 512]).then_inc(dve_chain, 1)
                chained[0] += 2
                dve.wait_ge(dve_chain, chained[0])
                link(nc.vector.bn_aggr(mv[:, par, :], bn[:, par, :]))
                nc.vector.tensor_scalar(mv[:, par, 1:2], mv[:, par, 1:2], EPS, None, ALU.add).then_inc(done, 1)

            def ln_shift(l, j, ln):
                dve.wait_ge(S[ln + "_pow"], BEFORE[l][ln + "_pow"] + j + 1)
                nc.vector.scalar_tensor_tensor(shift[:, j % 2, :], mv[:, j % 2, 0:1], -1.0, rs[:, j % 2, :], ALU.mult, ALU.mult).then_inc(S[ln + "_shift"], 1)

            def ln_weight(l, j, ln, ln_rows):
                dve.wait_ge(S[ln + "_act"], BEFORE[l][ln + "_act"] + j + 1)
                xt = X[:, tiles_of(l)[j], :]
                nc.vector.tensor_tensor(xt, xt, ln_rows[:, 0, :], ALU.mult).then_inc(S[ln + "_x"], 1)

            for l in range(DEPTH):
                s0, T = BEFORE[l], tiles_of(l)
                n = len(T)
                dve.wait_ge(S["small_in"], s0["small_in"] + 160)
                link(nc.vector.tensor_scalar(modc[:, 1, :, :], modc[:, 1, :, :], 1.0, None, ALU.add))
                nc.vector.tensor_scalar(modc[:, 3, :, :], modc[:, 3, :, :], 1.0, None, ALU.add).then_inc(S["one_added"], 1)
                transpose_in(l, 0)
                dve.wait_ge(S["rope_in"], s0["rope_in"] + 32)
                dve.wait_ge(S["dec_op"], s0["dec_op"] + 2)
                nc.vector.tensor_scalar(k_dec, k_dec_raw, K_SCALE, None, ALU.mult).then_inc(S["kdec_done"], 1)
                link(nc.vector.tensor_scalar(ident_s, ident, K_SCALE, None, ALU.mult))
                for h in range(HEADS):
                    link(nc.vector.tensor_scalar(masks[:, h, :], dist[:, 1, :], decay[:, 1, h:h + 1], None, ALU.mult))
                    last = nc.vector.scalar_tensor_tensor(masks[:, h, :], dist[:, 0, :], decay[:, 0, h:h + 1], masks[:, h, :], ALU.mult, ALU.add)
                    if h < HEADS - 1:
                        link(last)
                last.then_inc(S["mask_arg"], 1)
                dve.wait_ge(S["mask_exp"], s0["mask_exp"] + 1)
                link(nc.vector.scalar_tensor_tensor(masks, masks, K_SCALE, ident_s.unsqueeze(1).to_broadcast([P, HEADS, P]), ALU.mult, ALU.add))
                nc.vector.memset(u_t[:, :, 0:REACH], 0.0)
                mid = REACH + CTX_TILES * P
                nc.vector.memset(u_t[:, :, mid:mid + 2 * REACH], 0.0)
                link(nc.vector.memset(u_t[:, :, UT - REACH:UT], 0.0))
                steps, plan = PLANS[l]
                qn = [sum(st[0] == "Q" for st in steps[:i]) for i in range(len(steps) + 1)]
                runs = conv_ranges(l)
                R = len(runs)
                F_ORDER = list(range(NT))
                B_ORDER = [1, 0] + list(range(NT - 1, CTX_TILES - 1, -1))
                for a in plan:
                    if a[0] == "evac" and steps[a[1]][0] == "AB":
                        i = a[1]
                        ab = i - qn[i]
                        dve.wait_ge(S["sig_done"], s0["sig_done"] + ab + 1)
                        if ab >= 2:
                            prev = [k for k in range(i) if steps[k][0] == "AB"][ab - 2]
                            dve.wait_ge(S["post_done"], s0["post_done"] + prev + 1)
                        nc.vector.tensor_tensor(u_sb[:, ab % 2, :], ps_proj[i % 4][:, 0:2 * P], sig, ALU.mult).then_inc(S["glu_done"], 1)
                    elif a[0] == "scan":
                        p = a[1]
                        base = 2 * NT * p
                        dve.wait_ge(S["u_evac"], s0["u_evac"] + NT * (p + 1))
                        if p:
                            dve.wait_ge(S["sd_done"], s0["sd_done"] + n * p)
                        nc.vector.memset(state[:, F_ORDER[0], 0, :], 0.0).then_inc(S["scan_op"], 1)
                        nc.vector.memset(state[:, B_ORDER[0], 1, :], 0.0).then_inc(S["scan_op"], 1)
                        for k in range(1, NT):
                            for d, order in enumerate((F_ORDER, B_ORDER)):
                                dve.wait_ge(S["scan_op"], s0["scan_op"] + base + 2 * k + d - 1)
                                nc.vector.scalar_tensor_tensor(state[:, order[k], d, :], state[:, order[k - 1], d, :], c_dec[:, d, p:p + 1],
                                                               kv_u[:, order[k - 1], d, :], ALU.mult, ALU.add).then_inc(S["scan_op"], 1)
                    elif a[0] == "scores":
                        _, p, t = a
                        r = row_of(l, p, t)
                        dve.wait_ge(S["score_done"], s0["score_done"] + r + 1)
                        if r >= 2:
                            dve.wait_ge(S["val_done"], s0["val_done"] + r - 1)
                        nc.vector.tensor_tensor(probs[:, r % 2, :], ps_sc[:, 0:2 * P], masks[:, 2 * p:2 * p + 2, :].rearrange("p a b -> p (a b)"), ALU.mult).then_inc(S["prob_done"], 1)
                    elif a[0] == "values":
                        _, p, t = a
                        r = row_of(l, p, t)
                        dve.wait_ge(S["val_done"], s0["val_done"] + r + 1)
                        if r:
                            dve.wait_ge(S["comb_done"], s0["comb_done"] + r)
                        by_dir = inter.rearrange("p (h d e) -> p h d e", h=2, d=2)
                        nc.vector.tensor_tensor(inter.rearrange("p (a e) -> p a e", e=DK), ps_o[:, P:3 * P].rearrange("p (a e) -> p a e", e=DK),
                                                q_dec[:, 2 * p:2 * p + 2, :].rearrange("p a b -> p (a b)").unsqueeze(2).to_broadcast([P, 4, DK]), ALU.mult).then_inc(S["comb_a"], 1)
                        dve.wait_ge(S["comb_a"], s0["comb_a"] + r + 1)
                        nc.vector.tensor_tensor(by_dir[:, :, 0, :], ps_o[:, 0:P].rearrange("p (h e) -> p h e", h=2),
                                                by_dir[:, :, 0, :], ALU.add).then_inc(S["comb_b"], 1)
                        dve.wait_ge(S["comb_b"], s0["comb_b"] + r + 1)
                        if r >= 2:
                            dve.wait_ge(S["o_st"][r % 2], s0["o_st"] + 16 * (r // 2))
                        nc.vector.tensor_tensor(o_out[:, r % 2, :].rearrange("p (h e) -> p h e", h=2), by_dir[:, :, 0, :],
                                                by_dir[:, :, 1, :], ALU.add).then_inc(S["comb_done"], 1)
                    elif a[0] == "taps":
                        _, h, a0, a1 = a
                        if (h, a0) == (0, 0):
                            dve.wait_ge(S["conv_in"], s0["conv_in"] + 80)
                        if a0 == 0:
                            dve.wait_ge(S["post_evac"], s0["post_evac"] + 1 + max(k for k, st in enumerate(steps) if st[:2] == ("AB", h)))
                        for k in range(a0, a1):
                            ct, tap = k // TAPS, k % TAPS
                            if tap == 0 and h + ct:
                                dve.wait_ge(S["cv_st"], s0["cv_st"] + 16 * (2 * h + ct))
                            for r, (at, w, src) in enumerate(runs):
                                taps_in = u_t[:, ct, src + tap:src + tap + w]
                                wcol = cw[:, 2 * h + ct, tap:tap + 1]
                                if tap == 0:
                                    nc.vector.tensor_scalar(acc[:, at:at + w], taps_in, wcol, cb[:, 2 * h + ct:2 * h + ct + 1], ALU.mult, ALU.add).then_inc(S["conv_op"], 1)
                                else:
                                    dve.wait_ge(S["conv_op"], s0["conv_op"] + ((h * 2 * TAPS) + k) * R + r - R + 1)
                                    nc.vector.scalar_tensor_tensor(acc[:, at:at + w], taps_in, wcol, acc[:, at:at + w], ALU.mult, ALU.add).then_inc(S["conv_op"], 1)
                dve.wait_ge(S["rows_in"], s0["rows_in"] + 96)
                for st in range(n + 2):
                    if st < n:
                        t, par = T[st], st % 2
                        ps = banks[4 + par]
                        o = X[:, t, 0:512].rearrange("p (h e) -> p h e", h=HEADS)
                        xc = X[:, t, 512:D]
                        mean, var, rstd = (gstat[:, par, i * HEADS:(i + 1) * HEADS] for i in range(3))
                        dve.wait_ge(S["cvt_done"], s0["cvt_done"] + st + 1)
                        link(nc.vector.bn_stats(bn[:, par, 0:6], ps[:, :]))
                        link(nc.vector.bn_aggr(mv[:, par, :], bn[:, par, 0:6]))
                        nc.vector.tensor_scalar(mv[:, par, 1:2], mv[:, par, 1:2], EPS, None, ALU.add).then_inc(S["cn_var"], 1)
                        dve.wait_ge(S["o_in"][par], s0["o_in"] + 16 * (st // 2 + 1))
                        link(nc.vector.tensor_reduce(mean, o, AX.X, ALU.add))
                        link(nc.vector.tensor_scalar(mean, mean, 1.0 / DK, None, ALU.mult))
                        nc.vector.tensor_tensor(o, o, mean.unsqueeze(2).to_broadcast([P, HEADS, DK]), ALU.subtract).then_inc(S["gn_cent"], 1)
                        dve.wait_ge(S["sq_done"], s0["sq_done"] + st + 1)
                        link(nc.vector.tensor_reduce(var, sq.rearrange("p (h e) -> p h e", h=HEADS), AX.X, ALU.add))
                        nc.vector.tensor_scalar(var, var, 1.0 / DK, EPS, ALU.mult, ALU.add).then_inc(S["gn_var"], 1)
                        dve.wait_ge(S["cn_pow"], s0["cn_pow"] + st + 1)
                        nc.vector.tensor_scalar(xc, ps[:, :], mv[:, par, 0:1], rs[:, par, :], ALU.subtract, ALU.mult).then_inc(S["cnorm"], 1)
                        dve.wait_ge(S["cnorm"], s0["cnorm"] + st + 1)
                        link(nc.vector.tensor_tensor(xc, xc, rows[:, 2, :], ALU.mult))
                        nc.vector.tensor_tensor(xc, xc, rows[:, 3, :], ALU.add).then_inc(S["conv_aff"], 1)
                        dve.wait_ge(S["gn_pow"], s0["gn_pow"] + st + 1)
                        nc.vector.tensor_tensor(o, o, rstd.unsqueeze(2).to_broadcast([P, HEADS, DK]), ALU.mult).then_inc(S["gn_norm"], 1)
                    j = st - 1
                    if 0 <= j < n:
                        dve.wait_ge(S["mix_hi"], s0["mix_hi"] + j + 1)
                        cols = slice(T[j] * P, (T[j] + 1) * P)
                        for half in range(2):
                            last = nc.vector.tensor_tensor(x_lo[:, 4 * half:4 * half + 4, cols], banks[half][:, :].rearrange("p (a b) -> p a b", b=P),
                                                           x_hi[:, 4 * half:4 * half + 4, cols].bitcast(F32), ALU.subtract)
                        last.then_inc(S["mix_lo"], 1)
                    j = st - 2
                    if j >= 0:
                        dve.wait_ge(S["z_done"], s0["z_done"] + j + 1)
                        dve.wait_ge(S["res_in"][j % 2], s0["res_in"] + 16 * (j // 2 + 1))
                        nc.vector.tensor_tensor(z_t, banks[2 + j % 2][:, :], gate_row[:, cond_of(T[j]), :], ALU.mult).then_inc(S["z_read"], 1)
                        dve.wait_ge(S["z_read"], s0["z_read"] + j + 1)
                        link(nc.vector.scalar_tensor_tensor(X[:, T[j], 0:512], X[:, T[j], 0:512], ALPHA, z_t, ALU.mult, ALU.add))
                dve.wait_ge(S["gate_in"], s0["gate_in"] + 64)
                for st in range(n + 2):
                    if st < n:
                        dve.wait_ge(S["z_done"], s0["z_done"] + n + st + 1)
                        nc.vector.tensor_tensor(z_t, banks[2 + st % 2][:, :], g_in[:, cond_of(T[st]), :], ALU.mult).then_inc(S["z_read"], 1)
                        dve.wait_ge(S["z_read"], s0["z_read"] + n + st + 1)
                        link(nc.vector.scalar_tensor_tensor(X[:, T[st], 512:D], X[:, T[st], 512:D], ALPHA, z_t, ALU.mult, ALU.add))
                        row_stats(st % 2, T[st], S["ln_var"])
                    if 1 <= st <= n:
                        ln_shift(l, st - 1, "ln")
                    if st >= 2:
                        ln_weight(l, st - 2, "ln", ln1_rows)
                transpose_in(l, 1)
                dve.wait_ge(S["gate2_in"], s0["gate2_in"] + 32)
                dve.wait_ge(S["scaled"], s0["scaled"] + n)
                chunks = chunks_of(l)
                HB, YB = 2 * len(chunks), 2 * n

                def mlp_block(b, first, last=False):
                    for j in range(HB):
                        t0, nt = chunks[j // 2]
                        cols = slice(t0 * P, (t0 + nt) * P)
                        w = nt * P
                        a32 = act32[:, j % 2, 0:w]
                        dve.wait_ge(S["relu_done"], s0["relu_done"] + b * HB + (j + 1))
                        if j >= 2 or not first:
                            dve.wait_ge(S["h_split"], s0["h_split"] + b * HB + (j - 1))
                        rl = relu[:, j % 2, 0:w]
                        if nt == CTX_TILES:
                            nc.vector.tensor_tensor(rl, banks[j % 2][:, 0:w], rl, ALU.add).then_inc(S["ctx_sum"], 1)
                            dve.wait_ge(S["ctx_sum"], s0["ctx_sum"] + b * 2 + (j + 1))
                            nc.vector.scalar_tensor_tensor(a32, rl, 0.0, rl, ALU.max, ALU.mult).then_inc(S["h_sq"], 1)
                        else:
                            nc.vector.tensor_tensor(a32, rl, rl, ALU.mult).then_inc(S["h_sq"], 1)
                        dve.wait_ge(S["h_sq"], s0["h_sq"] + b * HB + (j + 1))
                        if j == 0 and not first:
                            dve.wait_ge(S["y_done"], s0["y_done"] + b * YB)
                        nc.vector.tensor_copy(h_hi[:, j % 2, cols], a32).then_inc(S["h_high"], 1)
                        dve.wait_ge(S["h_high"], s0["h_high"] + b * HB + (j + 1))
                        nc.vector.tensor_tensor(h_lo[:, j % 2, cols], a32, h_hi[:, j % 2, cols].bitcast(F32), ALU.subtract).then_inc(S["h_split"], 1)
                    for ti, t in enumerate(T):
                        for half in range(2):
                            yi = 2 * ti + half
                            hc = slice(half * 512, (half + 1) * 512)
                            dve.wait_ge(S["y_done"], s0["y_done"] + b * YB + (yi + 1))
                            if yi >= 2 or not first:
                                dve.wait_ge(S["y_add"], s0["y_add"] + b * YB + (yi - 1))
                            nc.vector.tensor_tensor(y_t[:, yi % 2, :], banks[2 + yi % 4][:, :], gate2[:, cond_of(t), hc], ALU.mult).then_inc(S["y_read"], 1)
                            dve.wait_ge(S["y_read"], s0["y_read"] + b * YB + (yi + 1))
                            nc.vector.tensor_tensor(X[:, t, hc], X[:, t, hc], y_t[:, yi % 2, :], ALU.add).then_inc(S["y_add"], 1)
                        if last:
                            dve.wait_ge(S["y_add"], s0["y_add"] + b * YB + 2 * (ti + 1))
                            row_stats(ti % 2, t, S["ln2_var"])
                            if ti >= 1:
                                ln_shift(l, ti - 1, "ln2")
                            if ti == 2:
                                dve.wait_ge(S["gate2_in"], s0["gate2_in"] + 64)
                            if ti >= 2:
                                ln_weight(l, ti - 2, "ln2", ln2_rows)

                mlp_block(0, True)
                with dve.Fori(1, NBLK - 1) as b:
                    mlp_block(b, False)
                mlp_block(NBLK - 1, False, last=True)
                ln_shift(l, n - 1, "ln2")
                ln_weight(l, n - 2, "ln2", ln2_rows)
                ln_weight(l, n - 1, "ln2", ln2_rows)


INPUTS = ["x", "c", "ctx", "c_ctx", "w_ada", "b_ada", "w_in", "ret_log_rate_fwd", "ret_log_rate_bwd",
          "ret_gn_w", "ret_gn_b", "conv_w", "conv_b", "conv_ln_w", "conv_ln_b", "w_out", "ln1_w", "ln1_b",
          "w_ff1", "w_ff2", "ln2_w", "ln2_b"]


def kernel(**inputs):
    import concourse.bacc as bacc
    from concourse.bass_utils import run_bass_kernel_spmd

    nc = bacc.Bacc("TRN2", target_bir_lowering=False, num_devices=1)
    arrays = {name: np.ascontiguousarray(inputs[name]) for name in INPUTS}
    arrays.update(shape_constants())
    args = [nc.dram_tensor(f"in_{name}", a.shape, mybir.dt.from_np(a.dtype), kind="ExternalInput").ap() for name, a in arrays.items()]
    out = nc.dram_tensor("out", (1, LAT_TILES * P, D), F32, kind="ExternalOutput").ap()
    build(nc, *args, out)
    result = run_bass_kernel_spmd(nc, [{f"in_{name}": a for name, a in arrays.items()}], core_ids=[0])
    return result.results[0]["out"]
```

```python
from contextlib import ExitStack

import numpy as np

import concourse.bass as bass
from concourse import mybir
from concourse.alu_op_type import AluOpType as ALU

F32 = mybir.dt.float32
F32R = mybir.dt.float32r
ACT = mybir.ActivationFunctionType
AX = mybir.AxisListType

P = 128
D = 1024
KT = D // P
DEPTH = 2
CTX_TILES, LAT_TILES = 2, 8
NT = CTX_TILES + LAT_TILES
NTOK = NT * P
HEADS, DK = 8, 64
PAIRS = HEADS // 2
CONV = 512
TAPS = 31
REACH = TAPS // 2
FF = 4 * D
IN_WIDTH = 6 * 512
GRID_W = 64
EPS = 1e-5
ALPHA = float((2 * DEPTH) ** 0.25)
K_SCALE = DK ** -0.5
UNIT = 1024
BLK = 256
NBLK = FF // BLK
RING = 6
IN_UNITS, OUT_UNITS = 24, 8
LAYER_UNITS = IN_UNITS + OUT_UNITS + 4 * NBLK
UT = REACH + CTX_TILES * P + 2 * REACH + LAT_TILES * P + REACH


def tiles_of(layer):
    return list(range(0 if layer < DEPTH - 1 else CTX_TILES, NT))


def chunks_of(layer):
    lat = [(CTX_TILES, 4), (CTX_TILES + 4, 4)]
    return ([(0, CTX_TILES)] if layer < DEPTH - 1 else []) + lat


GROUPS = [("AB", 0), ("Q", 0), ("Q", 1), ("AB", 1), ("Q", 2), ("Q", 3)]
TAPS_STEP = 3
ADA_BUFS = 4
ADA_FIRST, ADA_TAIL = 12, 6
ADA_LATE = 2


def mix_in_plan(layer):
    tiles = tiles_of(layer)
    steps = []
    first_of = {}
    for kind, i in GROUPS:
        first_of[kind, i] = len(steps)
        steps += [(kind, i, t) for t in (tiles if kind == "AB" else range(NT))]
    group_of = [GROUPS.index((kind, i)) for kind, i, _ in steps]
    sizes = [group_of.count(g) for g in range(len(GROUPS))]
    starts = [group_of.index(g) for g in range(len(GROUPS))]
    plan, evacs, posts, ready = [], list(range(len(steps))), list(range(len(steps))), []
    scored, valued, scanned, evac_at, taps = set(), set(), set(), {}, []
    n = 0
    ada = [(g, half) for g in range(ADA_FIRST + ADA_TAIL * layer, ADA_FIRST + ADA_TAIL * (layer + 1) - ADA_LATE) for half in range(2)]
    rows = []
    while n < len(steps) or posts or len(valued) < PAIRS * len(tiles) or ada or rows:
        if n < len(steps):
            plan.append(("proj", n))
            g, j = group_of[n], n - starts[group_of[n]]
            if j in (2, 5):
                plan.append(("load", 4 * (g + 1) + (j == 5)))
            if j == sizes[g] - 1:
                plan += [("load", 4 * (g + 1) + 2), ("load", 4 * (g + 1) + 3)]
            if steps[n][:2] == GROUPS[-1] and steps[n][2] in (5, 9):
                plan += [("ada_load", g, 4 if steps[n][2] == 5 else 8) for g, half in ada[:2 * ADA_BUFS] if half and g % ADA_BUFS // 2 == (steps[n][2] == 9)]
            if n == len(steps) - 1:
                plan += [("ada_bias_load", g) for g, half in ada[:2 * ADA_BUFS] if half]
        now = ready[:1] if ready and ready[0] in scored else []
        if n < len(steps):
            for p, t in now:
                plan.append(("values", p, t))
                valued.add(ready.pop(0))
            if ready:
                plan.append(("scores", *ready[0]))
                scored.add(ready[0])
        else:
            following = [x for x in ready if x not in scored][:1]
            for x in following:
                plan.append(("scores", *x))
                scored.add(x)
            if rows:
                g = rows.pop(0)
                plan.append(("ada_row", g))
                if g + ADA_BUFS < ADA_FIRST + ADA_TAIL * (layer + 1):
                    plan += [("ada_load", g + ADA_BUFS, NT), ("ada_bias_load", g + ADA_BUFS)]
            if ada and not evacs:
                plan.append(("ada", *ada[0]))
                g, half = ada.pop(0)
                if half:
                    rows.append(g)
            for p, t in now:
                plan.append(("values", p, t))
                valued.add(ready.pop(0))
        while evacs and evacs[0] <= n:
            kind, p, t = steps[evacs[0]]
            if kind == "Q" and p and t in tiles and (p - 1, t) not in valued:
                break
            plan.append(("evac", evacs[0]))
            evac_at[evacs.pop(0)] = n
        k = 0
        while posts and k < 2 and evac_at.get(posts[0], n) < n:
            kind, p, t = steps[posts[0]]
            plan.append(("post", posts.pop(0)))
            k += 1
            if t == NT - 1:
                if kind == "Q":
                    plan.append(("scan", p))
                    assert not p or all((p - 1, u) in valued for u in tiles)
                    ready += [(p, u) for u in tiles]
                else:
                    taps += [(p, a, min(a + TAPS_STEP, 2 * TAPS)) for a in range(0, 2 * TAPS, TAPS_STEP)]
        if taps:
            plan.append(("taps", *taps.pop(0)))
        if n == 3:
            plan.append(("masks",))
        n += 1
    assert not taps
    return steps, plan


def shape_constants():
    f = np.float32
    i = np.arange(P, dtype=f)
    dist = i[None, :] - i[:, None]
    cols = np.stack([-(i + 1), -(P - i), -(P - 1 - i), -i], axis=1)
    inv = np.power(f(10000.0), -(np.arange(DK // 4, dtype=f) / f(DK // 4))).astype(f)
    n = np.arange(LAT_TILES * P)
    row, col = (n // GRID_W).astype(f), (n % GRID_W).astype(f)
    ang = np.concatenate([row[:, None] * inv, col[:, None] * inv], axis=-1).astype(f)
    cos, sin = np.cos(ang), np.sin(ang)
    one = np.ones((CTX_TILES * P, DK // 2), f)
    rope = np.stack([np.concatenate([one, cos]), np.concatenate([0 * one, sin])], axis=1)
    rope = rope.reshape(NT, P, 2, DK // 2).transpose(1, 0, 2, 3)
    const = np.concatenate([np.eye(P, dtype=f), -np.maximum(dist, 0), -np.maximum(-dist, 0), cols], axis=1)
    return {"const_cols": np.ascontiguousarray(const, dtype=f),
            "const_rope": np.ascontiguousarray(rope, dtype=f)}


def layer_counts(l):
    n = len(tiles_of(l))
    runs = len(chunks_of(l))
    conv_tiles, q_tiles, ret_steps = 2 * n, PAIRS * NT, PAIRS * n
    t_in, t_mlp = (1 + runs if l else runs) * KT, runs * KT
    hidden, shares = 2 * runs * NBLK, 2 * n * NBLK
    each = {
        1: "kdec_done mask_arg mask_exp zero_set",
        2: "dec_op one_added",
        n: "scaled cvt_done cnorm cn_var cn_pow conv_aff gn_cent gn_var gn_pow gn_norm mix_a mix_b mixtr_done "
           "cn_shift mix_hi mix_lo silu_g sq_done ln_var ln_pow ln_shift ln_act ln1_done ln2_var ln2_pow ln2_shift "
           "ln2_act ln2_done",
        n // 2: "ln_x ln_own ln2_x ln2_own",
    }
    counts = {name: k for k, names in each.items() for name in names.split()}
    counts.update(
        x_in=0 if l else 32, small_in=96, mod2_in=64, conv_in=80, rope_in=32, rows_in=96, gate_in=64, gate2_in=64, cv_st=64,
        tr_in=t_in + t_mlp, hi_in=t_in + t_mlp, mod_in=t_in + t_mlp, split_in=t_in + t_mlp, gn_aff=2 * n,
        proj_done=conv_tiles + q_tiles, post_done=conv_tiles + q_tiles, post_evac=conv_tiles + q_tiles,
        sig_done=conv_tiles, glu_done=conv_tiles, conv_op=4 * TAPS * runs, scan_op=2 * NT * PAIRS,
        rot_part=4 * q_tiles, rot_done=2 * q_tiles,
        z_done=2 * n, z_read=2 * n)
    for name in "qk_ready v_ready evac_q vdec_done u_done u_evac".split():
        counts[name] = q_tiles
    for name in "qd_done sd_done score_done prob_done val_done comb_a comb_b comb_done".split():
        counts[name] = ret_steps
    for name in "h_done relu_done h_sq h_high h_split".split():
        counts[name] = hidden
    for name in "y_done y_read y_add".split():
        counts[name] = shares
    pairs = {"g_st": 8 * q_tiles, "o_st": 8 * ret_steps}
    pairs.update({name: 8 * n for name in "o_in g_in cv_in res_in".split()})
    return counts, pairs


def build(nc, x, c, ctx, c_ctx, w_ada, b_ada, w_in, rate_f, rate_b, gn_w, gn_b, conv_w, conv_b,
          cln_w, cln_b, w_out, ln1_w, ln1_b, w_ff1, w_ff2, ln2_w, ln2_b, const_cols, const_rope, out):
    es = ExitStack()
    with es:
        es.enter_context(nc.allow_non_contiguous_dma(reason="small per-channel columns"))

        def sb(name, shape, dt=F32):
            return es.enter_context(nc.sbuf_tensor(name, shape, dt))

        def sem(name):
            return es.enter_context(nc.semaphore(name))

        ada_d = nc.dram_tensor("ada_rows", (DEPTH, 2, 6 * D), F32, kind="Internal").ap()
        o_d = nc.dram_tensor("retention_rows", (DEPTH, NTOK, 512), F32, kind="Internal").ap()
        g_d = nc.dram_tensor("gate_rows", (DEPTH, NTOK, 512), F32, kind="Internal").ap()
        cv_d = nc.dram_tensor("conv_columns", (DEPTH, 4, P, NTOK), F32, kind="Internal").ap()
        x_d = nc.dram_tensor("residual_rows", (LAT_TILES * P, D), F32, kind="Internal").ap()

        with nc.sbuf_tensor("plain_words", [P, 2, KT, NTOK], F32) as plain:
            pass
        x_hl = sb("x_hl", [P, 2, KT, NTOK], F32R)
        x_hi, x_lo = x_hl[:, 0], x_hl[:, 1]
        w_hi = sb("w_hi", [P, 4, UNIT], F32R)
        w_lo = sb("w_lo", [P, 4, UNIT], F32R)
        h_hi = sb("h_hi", [P, 2, NTOK], F32R)
        h_lo = sb("h_lo", [P, 2, NTOK], F32R)
        raw = sb("raw", [P, 2, UNIT])
        KEEP, Y_SIZE = 656, 6400
        WORK = KEEP + NT * D + Y_SIZE
        work = sb("work", [P, WORK])

        def carver(at, limit):
            state = [at]

            def take(*shape):
                n = int(np.prod(shape))
                piece = work[:, state[0]:state[0] + n]
                state[0] += n
                assert state[0] <= limit, (state[0], limit)
                if len(shape) == 2:
                    piece = piece.rearrange("p (a b) -> p a b", b=shape[1])
                elif len(shape) == 3:
                    piece = piece.rearrange("p (a b c) -> p a b c", b=shape[1], c=shape[2])
                return piece
            return take

        keep = carver(0, KEEP)
        ident = keep(P)
        expo = keep(4)
        neg_half = keep(16)
        decay = keep(2, HEADS)
        q_dec = keep(HEADS, 2)
        k_dec = keep(HEADS, 2)
        k_dec_raw = keep(HEADS, 2)
        c_dec = keep(2, PAIRS)
        cw = keep(4, TAPS)
        cb = keep(4)
        modc = keep(4, 2, KT)
        bn = keep(2, 12)
        mv = keep(2, 2)
        rs = keep(2, 1)
        shift = keep(2, 1)
        cond = keep(KT, 2)
        cond_s = keep(KT, 2)
        gstat = keep(2, 3 * HEADS)
        XA = KEEP
        YA = XA + NT * D
        X = work[:, XA:YA].rearrange("p (t d) -> p t d", d=D)

        m = carver(XA, WORK)
        v_sb = m(NT, P)
        qk_t = m(NT, 2, P)
        kv_u = m(NT, 2, DK)
        state = m(NT, 2, DK)
        u_t = m(2, UT)
        acc = m(NTOK)
        rope = m(NT, 2, DK // 2)
        masks = m(HEADS, P)
        qk_raw = m(2, 2 * P)
        qk_rot = m(2, 2 * P)
        rot_tmp = m(2 * P)
        v_dec = m(2 * P)
        g_out = m(2, P)
        probs = m(2, 2 * P)
        diag_both = m(8 * P)
        q_diag = diag_both[:, 0:4 * P].rearrange("p (a b) -> p a b", a=2)
        s_diag = diag_both[:, 4 * P:].rearrange("p (a b) -> p a b", a=2)
        inter = m(2 * P)
        o_out = m(2, P)
        sig = m(2 * P)
        u_sb = m(2, 2 * P)
        dist = inter.rearrange("p (a b) -> p a b", b=P)
        ident_s = o_out[:, 0, :]

        mod32 = carver(YA + 4096, WORK)(2, 512)
        y = carver(YA, WORK)
        rows = y(4, 512)
        gate_row = y(2, 512)
        g_in = y(2, 512)
        cv_in = y(2, 4, P)
        sq = y(512)
        z_t = y(512)
        ln1_rows = work[:, YA:YA + 2 * D].rearrange("p (a b) -> p a b", b=D)
        y = carver(YA, WORK)
        gate2 = y(2, D)
        relu = y(2, 512)
        act32 = y(2, 512)
        y_t = y(2, 512)
        ln2_rows = work[:, YA + 2 * D:YA + 4 * D].rearrange("p (a b) -> p a b", b=D)
        ada_w = [plain[:, i % 2, :, (i // 2) * 512:(i // 2) * 512 + 512] for i in range(ADA_BUFS)]
        ada_b = [plain[0:2, 0, 2 * i:2 * i + 2, 2 * 512:NTOK] for i in range(ADA_BUFS)]
        ada_o = [plain[0:2, 1, 2 * i:2 * i + 2, 2 * 512:NTOK] for i in range(2)]

        banks = [es.enter_context(nc.psum_tensor(f"bank{i}", [P, 512], F32)) for i in range(8)]
        ps_proj = banks[0:4]
        ps_tr, ps_u, ps_sc, ps_o = banks[4:8]

        raw_in = [sem(f"raw_in{i}") for i in range(2)]
        w_high, w_ready, w_used = sem("w_high"), sem("w_ready"), sem("w_used")
        const_in, half_set = sem("const_in"), sem("half_set")
        cond_in, cond_ready = sem("cond_in"), sem("cond_ready")
        adaw_in = [sem(f"adaw_in{i}") for i in range(ADA_BUFS)]
        ada_st = [sem(f"ada_st{i}") for i in range(2)]
        ada_done, ada_row = sem("ada_done"), sem("ada_row")
        dve_chain, out_st = sem("dve_chain"), sem("out_st")
        x_st = sem("x_st")

        counts, pairs = layer_counts(0)
        S = {name: sem(name) for name in counts}
        S.update({name: [sem(f"{name}{i}") for i in range(2)] for name in pairs})

        def counted_before(l):
            base = {name: 0 for name in S}
            for before in range(l):
                for part in layer_counts(before):
                    for name, count in part.items():
                        base[name] += count
            return base

        BEFORE = [counted_before(l) for l in range(DEPTH)]
        PLANS = [mix_in_plan(l) for l in range(DEPTH)]

        def unit_parts(l, u):
            if u < IN_UNITS:
                kind, i = GROUPS[u // 4]
                parts = []
                for kk in range(2):
                    k = 2 * (u % 4) + kk
                    w = w_in[l, k * P:(k + 1) * P, :]
                    if kind == "Q":
                        src = w[:, 0:4 * 512].rearrange("p (s c) -> p s c", s=4)[:, :, i * P:(i + 1) * P]
                    else:
                        src = w[:, 4 * 512:].rearrange("p (s c) -> p s c", s=2)[:, :, i * 2 * P:(i + 1) * 2 * P]
                    parts.append((slice(kk * 512, kk * 512 + 512), src))
                return parts
            u -= IN_UNITS
            if u < OUT_UNITS:
                k = 2 * (u % 4)
                src = w_out[l, k * P:(k + 2) * P, (u // 4) * 512:(u // 4 + 1) * 512]
                return [(slice(0, UNIT), src.rearrange("(k p) n -> p k n", p=P))]
            u -= OUT_UNITS
            return mlp_unit_parts(l, u // 4, u % 4)

        def mlp_unit_parts(l, b, s):
            if s < 2:
                src = w_ff1[l, :, bass.ds(b * BLK + s * P, P)].rearrange("(k p) n -> p k n", p=P)
            else:
                src = w_ff2[l, bass.ds(b * BLK + (s - 2) * P, P), :]
            return [(slice(0, UNIT), src)]

        def fetch(act, parity, parts):
            for cols, src in parts:
                dst = raw[:, parity, cols]
                if len(src.shape) == 3:
                    dst = dst.rearrange("p (a b) -> p a b", b=src.shape[2])
                act.dma_start(dst, src).then_inc(raw_in[parity], 32 // len(parts))

        def slot(s, part):
            if s < 4:
                return (w_hi, w_lo)[part][:, s, :]
            return (h_hi, h_lo)[part][:, :, :].rearrange("p a b -> p (a b)")[:, (s - 4) * UNIT:(s - 3) * UNIT]

        def mlp_slot(place):
            return (place + 2) % 4

        def slot_of(u):
            return u % RING if u < IN_UNITS + OUT_UNITS else mlp_slot(u - IN_UNITS - OUT_UNITS)

        def unit_released(eng, l, u):
            s0, g = BEFORE[l], u // 4
            if u % 4 < 3:
                eng.wait_ge(w_used, (3 * 8 * l) + 3 * g + u % 4 + 1)
            elif u < IN_UNITS:
                eng.wait_ge(S["proj_done"], s0["proj_done"] + 1 + max(n for n, st in enumerate(PLANS[l][0]) if GROUPS.index(st[:2]) == g))
            else:
                eng.wait_ge(S["z_done"], s0["z_done"] + (g - 5) * len(tiles_of(l)))

        def slot_free(eng, l, u):
            n_in = IN_UNITS + OUT_UNITS
            if u < RING:
                if l:
                    eng.wait_ge(S["y_done"], BEFORE[l - 1]["y_done"] + 2 * len(tiles_of(l - 1)) * NBLK)
            elif u < n_in:
                unit_released(eng, l, u - RING)
            else:
                unit_released(eng, l, {0: n_in - 6, 1: n_in - 5, 2: n_in - 2, 3: n_in - 1}[u - n_in])

        def split_high(act, l, u, following):
            un = l * LAYER_UNITS + u
            act.wait_ge(raw_in[un % 2], 32 * (un // 2 + 1))
            slot_free(act, l, u)
            nc.scalar.activation(slot(slot_of(u), 0), raw[:, un % 2, :], ACT.Copy).then_inc(w_high, 1)
            if following is not None:
                if un:
                    act.wait_ge(w_ready, un)
                fetch(act, (un + 1) % 2, unit_parts(*following))

        def next_unit(l, u):
            if u + 1 < LAYER_UNITS:
                return (l, u + 1)
            return (l + 1, 0) if l + 1 < DEPTH else None

        def split_low(pool, l, u):
            un = l * LAYER_UNITS + u
            pool.wait_ge(w_high, un + 1)
            s = slot_of(u)
            nc.gpsimd.tensor_tensor(slot(s, 1), raw[:, un % 2, :], slot(s, 0).bitcast(F32), ALU.subtract).then_inc(w_ready, 1)

        def three_passes(out_ps, hi, lo, whi, wlo, first, last):
            nc.tensor.matmul(out_ps, hi, whi, start=first, stop=False)
            nc.tensor.matmul(out_ps, hi, wlo, start=False, stop=False)
            return nc.tensor.matmul(out_ps, lo, whi, start=False, stop=last)

        def project(pe, l, u0, t, out_ps, first_tile, last_tile, done):
            cols = slice(t * P, (t + 1) * P)
            for k in range(KT):
                u = u0 + k // 2
                if first_tile and k % 2 == 0:
                    pe.wait_ge(w_ready, l * LAYER_UNITS + u + 1)
                wc = slice((k % 2) * 512, (k % 2) * 512 + 512)
                s = slot_of(u)
                mm = three_passes(out_ps, x_hi[:, k, cols], x_lo[:, k, cols], slot(s, 0)[:, wc], slot(s, 1)[:, wc],
                                  k == 0, k == KT - 1)
                if last_tile and k in (1, 3, 5):
                    mm.then_inc(w_used, 1)
            mm.then_inc(done, 1)

        def in_chunks(l, which):
            chunks = [(0, CTX_TILES)] + chunks_of(DEPTH - 1) if which == 0 else chunks_of(l)
            return [(t0, n, k) for t0, n in chunks for k in range(KT)]

        N_IN0 = len(in_chunks(0, 0))

        def share_bank(l, i):
            order = (6, 2, 3, 4, 5) if 2 * len(tiles_of(l)) % 5 == 0 else (2, 3, 4, 5)
            return banks[order[i % len(order)]]

        def share_banks(l):
            return 5 if 2 * len(tiles_of(l)) % 5 == 0 else 4

        def tr_bank(which, j):
            return banks[((6, 7), (6, 7, 4, 5))[which][j % (4 if which else 2)]]

        def by_vector(ln, j):
            return j % 2 == 1

        def beside_ln1(l):
            T, k, turns = tiles_of(l), 0, []
            items = in_chunks(l, 1)
            for turn in range(len(T) + 2):
                turns.append([])
                room = 8 if turn <= len(T) else KT * CTX_TILES * 2
                while k < len(items) - KT and T.index(items[k][0] + items[k][1] - 1) + 4 <= turn and sum(items[i][1] for i in turns[-1]) < room:
                    turns[-1].append(k)
                    k += 1
            assert k == len(items) - KT
            return turns

        def ada_bank(g):
            return banks[g % 2 + (6 if g < ADA_FIRST or g % ADA_TAIL >= ADA_TAIL - ADA_LATE else 0)][0:2, :].rearrange("p (a n) -> p a n", a=2)

        def ada_load(eng, g):
            l, j, buf = g // 12, g % 12, g % ADA_BUFS
            eng.dma_start(ada_w[buf], w_ada[l, :, j * 512:(j + 1) * 512].rearrange("(k p) n -> p k n", p=P)).then_inc(adaw_in[buf], 16)

        def ada_bias_load(eng, g):
            l, j, buf = g // 12, g % 12, g % ADA_BUFS
            eng.dma_start(ada_b[buf], b_ada[l, j * 512:(j + 1) * 512].partition_broadcast(2).rearrange("p (a n) -> p a n", a=2)).then_inc(adaw_in[buf], 16)

        def ada_products(pe, g, half):
            if half == 0:
                pe.wait_ge(adaw_in[g % ADA_BUFS], 32 * (g // ADA_BUFS + 1))
                if g >= 2:
                    pe.wait_ge(ada_row, g - 1)
            for k in range(4 * half, 4 * half + 4):
                mm = nc.tensor.matmul(ada_bank(g), cond_s[:, k, :], ada_w[g % ADA_BUFS][:, k, :].rearrange("p (a n) -> p a n", a=2),
                                      start=k == 0, stop=k == KT - 1)
            if half:
                mm.then_inc(ada_done, 1)

        def cond_of(t):
            return 1 if t < CTX_TILES else 0

        def ln_source_ready(eng, l, which, t_last):
            if which:
                eng.wait_ge(S["ln1_done"], BEFORE[l]["ln1_done"] + tiles_of(l).index(t_last) + 1)
            elif l:
                eng.wait_ge(S["ln2_done"], BEFORE[l - 1]["ln2_done"] + tiles_of(l - 1).index(t_last) + 1)
            else:
                eng.wait_ge(S["x_in"], BEFORE[0]["x_in"] + 32)

        def conv_ranges(l):
            lat = 2 * REACH + CTX_TILES * P
            runs = [(CTX_TILES * P, 512, lat), (CTX_TILES * P + 512, 512, lat + 512)]
            return ([(0, CTX_TILES * P, 0)] if l < DEPTH - 1 else []) + runs

        def row_of(l, p, t):
            T = tiles_of(l)
            return p * len(T) + T.index(t)

        block = es.enter_context(nc.Block())

        @block.sync
        def _(sp):
            sp.dma_start(ident, const_cols[:, 0:P]).then_inc(const_in, 16)
            sp.dma_start(expo, const_cols[:, 3 * P:3 * P + 4]).then_inc(const_in, 16)
            sp.dma_start(cond[:, :, 0], c.rearrange("a (k p) -> p (a k)", p=P)).then_inc(cond_in, 16)
            sp.dma_start(cond[:, :, 1], c_ctx.rearrange("(k p) -> p k", p=P)).then_inc(cond_in, 16)

            def ada_store(g):
                sp.wait_ge(ada_row, g + 1)
                l, j = g // 12, g % 12
                sp.dma_start(ada_d[l, :, j * 512:(j + 1) * 512].rearrange("c (a n) -> c a n", a=2), ada_o[g % 2]).then_inc(ada_st[g % 2], 16)

            def ada_stored(groups):
                for par in range(2):
                    sp.wait_ge(ada_st[par], 16 * (groups // 2))

            def modulation(l, which, done):
                for i, sec in enumerate((0, 1, 3, 4)[2 * which:2 * which + 2]):
                    for cd in range(2):
                        sp.dma_start(modc[:, 2 * which + i, cd, :], ada_d[l, cd, sec * D:(sec + 1) * D].rearrange("(k p) -> p k", p=P)).then_inc(done, 16)

            def small_loads(l):
                for d, rate in enumerate((rate_f, rate_b)):
                    sp.dma_start(decay[:, d, :], rate[l].partition_broadcast(P)).then_inc(S["small_in"], 16)
                modulation(l, 0, S["small_in"])
                sp.dma_start(cb, conv_b[l].rearrange("(k p) -> p k", p=P)).then_inc(S["conv_in"], 16)
                for ct in range(4):
                    sp.dma_start(cw[:, ct, :], conv_w[l, :, ct * P:(ct + 1) * P].rearrange("w p -> p w")).then_inc(S["conv_in"], 16)

            for g in range(ADA_FIRST):
                if g >= ADA_BUFS:
                    sp.wait_ge(ada_row, g - ADA_BUFS + 1)
                ada_load(sp, g)
                ada_bias_load(sp, g)
                if g == ADA_BUFS:
                    sp.dma_start(X[:, 0:CTX_TILES, :], ctx.rearrange("a (t p) d -> p (a t) d", p=P)).then_inc(S["x_in"], 16)
                    sp.dma_start(X[:, CTX_TILES:, :], x.rearrange("a (t p) d -> p (a t) d", p=P)).then_inc(S["x_in"], 16)
                if g >= ADA_BUFS:
                    ada_store(g - ADA_BUFS)
            for g in range(ADA_FIRST - ADA_BUFS, ADA_FIRST):
                ada_store(g)
            ada_stored(ADA_FIRST)

            for l in range(DEPTH):
                s0, T = BEFORE[l], tiles_of(l)
                n = len(T)
                if l == 0:
                    small_loads(l)
                else:
                    for i, (t0, nt) in enumerate(chunks_of(DEPTH - 1)):
                        ln_source_ready(sp, l, 0, t0 + nt - 1)
                        rows_at = slice((t0 - CTX_TILES) * P, (t0 - CTX_TILES + nt) * P)
                        sp.dma_start(x_d[rows_at, :].rearrange("(t p) d -> p t d", p=P), X[:, t0:t0 + nt, :]).then_inc(x_st, 16)
                sp.wait_ge(S["split_in"], s0["split_in"] + N_IN0)
                if l:
                    sp.wait_ge(x_st, 32)
                sp.dma_start(dist, const_cols[:, P:3 * P].rearrange("p (a b) -> p a b", b=P)).then_inc(S["rope_in"], 16)
                sp.dma_start(rope, const_rope).then_inc(S["rope_in"], 16)
                steps, plan = PLANS[l]
                q = 0
                R = len(conv_ranges(l))
                for a in plan:
                    if a[0] == "evac" and steps[a[1]][0] == "Q":
                        _, p, t = steps[a[1]]
                        sp.wait_ge(S["evac_q"], s0["evac_q"] + q + 1)
                        sp.dma_start(g_d[l, t * P:(t + 1) * P, p * P:(p + 1) * P], g_out[:, q % 2, :]).then_inc(S["g_st"][q % 2], 16)
                        q += 1
                    if a[0] == "values":
                        _, p, t = a
                        r = row_of(l, p, t)
                        sp.wait_ge(S["comb_done"], s0["comb_done"] + r + 1)
                        sp.dma_start(o_d[l, t * P:(t + 1) * P, p * P:(p + 1) * P], o_out[:, r % 2, :]).then_inc(S["o_st"][r % 2], 16)
                    if a[0] == "taps":
                        _, h, a0, a1 = a
                        for ct in range(2):
                            if a0 <= (ct + 1) * TAPS - 1 < a1:
                                sp.wait_ge(S["conv_op"], s0["conv_op"] + (h * 2 + ct + 1) * TAPS * R)
                                c0 = conv_ranges(l)[0][0]
                                sp.dma_start(cv_d[l, 2 * h + ct, :, c0:], acc[:, c0:]).then_inc(S["cv_st"], 16)
                    if a[0] == "ada_row":
                        ada_store(a[1])
                ada_all = ADA_FIRST + ADA_TAIL * (l + 1)
                ada_stored(ada_all - ADA_LATE)
                for par in range(2):
                    sp.wait_ge(S["g_st"][par], s0["g_st"] + 16 * (NT * PAIRS // 2))
                    sp.wait_ge(S["o_st"][par], s0["o_st"] + 16 * (n * PAIRS // 2))
                sp.wait_ge(S["cv_st"], s0["cv_st"] + 64)

                def residual(j):
                    t = T[j]
                    sp.wait_ge(S["mixtr_done"], s0["mixtr_done"] + j + 1)
                    if j >= 2:
                        sp.wait_ge(S["z_read"], s0["z_read"] + j - 1)
                    if l:
                        src = x_d[(t - CTX_TILES) * P:(t - CTX_TILES + 1) * P, :]
                    elif t < CTX_TILES:
                        src = ctx[0, t * P:(t + 1) * P, :]
                    else:
                        src = x[0, (t - CTX_TILES) * P:(t - CTX_TILES + 1) * P, :]
                    sp.dma_start(X[:, t, :], src).then_inc(S["res_in"][j % 2], 16)

                for j in range(n):
                    t = T[j]
                    if j >= 2:
                        sp.wait_ge(S["mix_a"], s0["mix_a"] + j - 1)
                        sp.wait_ge(S["cvt_done"], s0["cvt_done"] + j - 1)
                    sp.dma_start(X[:, t, 0:512], o_d[l, t * P:(t + 1) * P, :]).then_inc(S["o_in"][j % 2], 16)
                    sp.dma_start(g_in[:, j % 2, :], g_d[l, t * P:(t + 1) * P, :]).then_inc(S["g_in"][j % 2], 16)
                    sp.dma_start(cv_in[:, j % 2, :, :], cv_d[l, :, :, t * P:(t + 1) * P].rearrange("c p n -> p c n")).then_inc(S["cv_in"][j % 2], 16)
                    if j == 3:
                        for g in range(ada_all - ADA_LATE, ada_all):
                            ada_store(g)
                        ada_stored(ada_all)
                    if j == 1:
                        for i, r in enumerate((gn_w, gn_b, cln_w, cln_b)):
                            sp.dma_start(rows[:, i, :], r[l].partition_broadcast(P)).then_inc(S["rows_in"], 16)
                        for cd in range(2):
                            sp.dma_start(gate_row[:, cd, :], ada_d[l, cd, 2 * D:2 * D + 512].partition_broadcast(P)).then_inc(S["rows_in"], 16)
                        modulation(l, 1, S["mod2_in"])
                    if j >= 2:
                        residual(j - 2)
                residual(n - 2)
                residual(n - 1)
                for cd in range(2):
                    sp.dma_start(g_in[:, cd, :], ada_d[l, cd, 2 * D + 512:3 * D].partition_broadcast(P)).then_inc(S["gate_in"], 16)
                for i, r in enumerate((ln1_w, ln1_b)):
                    sp.dma_start(ln1_rows[:, i, :], r[l].partition_broadcast(P)).then_inc(S["gate_in"], 16)
                sp.wait_ge(S["ln1_done"], s0["ln1_done"] + n)
                for cd in range(2):
                    sp.dma_start(gate2[:, cd, :], ada_d[l, cd, 5 * D:6 * D].partition_broadcast(P)).then_inc(S["gate2_in"], 16)
                sp.wait_ge(S["h_split"], s0["h_split"] + 2 * len(chunks_of(l)) * NBLK)
                for i, r in enumerate((ln2_w, ln2_b)):
                    sp.dma_start(ln2_rows[:, i, :], r[l].partition_broadcast(P)).then_inc(S["gate2_in"], 16)
                if l + 1 < DEPTH:
                    small_loads(l + 1)
                if l == DEPTH - 1:
                    for j, t in enumerate(T):
                        sp.wait_ge(S["ln2_done"], s0["ln2_done"] + j + 1)
                        sp.dma_start(out[0, (t - CTX_TILES) * P:(t - CTX_TILES + 1) * P, :], X[:, t, :]).then_inc(out_st, 16)
            sp.wait_ge(out_st, 16 * LAT_TILES)

        @block.tensor
        def _(pe):
            pe.wait_ge(cond_ready, 1)
            for g in range(ADA_FIRST):
                for half in range(2):
                    ada_products(pe, g, half)

            def transpose_step(l, which, j):
                s0, base = BEFORE[l], N_IN0 * which
                t0, n, k = in_chunks(l, which)[j]
                if k == 0:
                    ln_source_ready(pe, l, which, t0 + n - 1)
                nb = 4 if which else 2
                if j >= nb:
                    pe.wait_ge(S["mod_in"], s0["mod_in"] + base + j - nb + 1)
                for i in range(n):
                    mm = nc.tensor.transpose(tr_bank(which, j)[:, i * P:(i + 1) * P], X[:, t0 + i, k * P:(k + 1) * P], ident)
                mm.then_inc(S["tr_in"], 1)

            pe.wait_ge(ada_row, ADA_FIRST)

            for l in range(DEPTH):
                s0, T = BEFORE[l], tiles_of(l)
                n = len(T)
                steps, plan = PLANS[l]
                qn = [sum(st[0] == "Q" for st in steps[:i]) for i in range(len(steps) + 1)]

                def project_step(i):
                    kind, p, t = steps[i]
                    g = GROUPS.index((kind, p))
                    project(pe, l, 4 * g, t, ps_proj[i % 4][:, :], i == 0 or steps[i - 1][:2] != steps[i][:2],
                            i + 1 == len(steps) or steps[i + 1][:2] != steps[i][:2], S["proj_done"])

                if l:
                    pe.wait_ge(S["y_read"], s0["y_read"])
                for j in range(2 * KT):
                    transpose_step(l, 0, j)
                pe.wait_ge(S["split_in"], s0["split_in"] + 2 * KT)
                for i in range(4):
                    project_step(i)
                    for j in range(2 * KT + 4 * i, min(2 * KT + 4 * i + 4, N_IN0)):
                        transpose_step(l, 0, j)
                pe.wait_ge(S["split_in"], s0["split_in"] + N_IN0)
                pe.wait_ge(S["zero_set"], s0["zero_set"] + 1)
                for a in plan:
                    if a[0] == "proj":
                        i = a[1]
                        if i < 4:
                            continue
                        if steps[i - 4][0] == "Q":
                            pe.wait_ge(S["evac_q"], s0["evac_q"] + qn[i - 3])
                        else:
                            pe.wait_ge(S["glu_done"], s0["glu_done"] + i - 3 - qn[i - 3])
                        project_step(i)
                    elif a[0] == "post":
                        i = a[1]
                        kind, p, t = steps[i]
                        if i:
                            pe.wait_ge(S["post_evac"], s0["post_evac"] + i)
                        if kind == "AB":
                            pe.wait_ge(S["glu_done"], s0["glu_done"] + i - qn[i] + 1)
                            src = u_sb[:, (i - qn[i]) % 2, :]
                        else:
                            pe.wait_ge(S["rot_done"], s0["rot_done"] + 2 * (qn[i] + 1))
                            src = qk_rot[:, qn[i] % 2, :]
                        for h in range(2):
                            mm = nc.tensor.transpose(ps_tr[:, h * P:(h + 1) * P], src[:, h * P:(h + 1) * P], ident)
                        mm.then_inc(S["post_done"], 1)
                        if kind == "Q":
                            pe.wait_ge(S["vdec_done"], s0["vdec_done"] + qn[i] + 1)
                            if qn[i]:
                                pe.wait_ge(S["u_evac"], s0["u_evac"] + qn[i])
                            nc.tensor.matmul(ps_u[:, 0:2 * P], src[:, P:2 * P], v_dec, start=True, stop=True).then_inc(S["u_done"], 1)
                    elif a[0] == "scores":
                        _, p, t = a
                        r = row_of(l, p, t)
                        pe.wait_ge(S["qd_done"], s0["qd_done"] + r + 1)
                        if r:
                            pe.wait_ge(S["prob_done"], s0["prob_done"] + r)
                        nc.tensor.matmul(ps_sc[:, 0:2 * P], qk_t[:, t, 1, :], q_diag[:, r % 2, :], start=True, stop=True).then_inc(S["score_done"], 1)
                    elif a[0] == "values":
                        _, p, t = a
                        r = row_of(l, p, t)
                        pe.wait_ge(S["prob_done"], s0["prob_done"] + r + 1)
                        pe.wait_ge(S["sd_done"], s0["sd_done"] + r + 1)
                        if r:
                            pe.wait_ge(S["comb_b"], s0["comb_b"] + r)
                        for h in range(2):
                            nc.tensor.matmul(ps_o[:, h * DK:(h + 1) * DK], probs[:, r % 2, h * P:(h + 1) * P], v_sb[:, t, h * DK:(h + 1) * DK], start=True, stop=True)
                        nc.tensor.matmul(ps_o[:, P:3 * P], qk_t[:, t, 0, :], s_diag[:, r % 2, :], start=True, stop=True).then_inc(S["val_done"], 1)
                    elif a[0] == "ada":
                        _, g, half = a
                        if g % ADA_TAIL == 0 and not half:
                            pe.wait_ge(S["evac_q"], s0["evac_q"] + NT * PAIRS)
                        ada_products(pe, g, half)
                ps_c, ps_z, ps_m = banks[4:6], banks[2:4], banks[0:2]
                for st in range(n + 3):
                    if st < n:
                        pe.wait_ge(S["cv_in"][st % 2], s0["cv_in"] + 16 * (st // 2 + 1))
                        if st >= 2:
                            pe.wait_ge(S["cnorm"], s0["cnorm"] + st - 1)
                        elif st == 0:
                            pe.wait_ge(S["post_evac"], s0["post_evac"] + len(steps))
                            pe.wait_ge(S["u_evac"], s0["u_evac"] + NT * PAIRS)
                        for ct in range(4):
                            mm = nc.tensor.transpose(ps_c[st % 2][:, ct * P:(ct + 1) * P], cv_in[:, st % 2, ct, :], ident)
                        mm.then_inc(S["cvt_done"], 1)
                        if st < ADA_LATE:
                            if st == 0:
                                pe.wait_ge(S["prob_done"], s0["prob_done"] + n * PAIRS)
                                pe.wait_ge(S["comb_b"], s0["comb_b"] + n * PAIRS)
                            for half in range(2):
                                ada_products(pe, ADA_FIRST + ADA_TAIL * (l + 1) - ADA_LATE + st, half)
                    j = st - 3
                    if j >= 0:
                        pe.wait_ge(S["mix_lo"], s0["mix_lo"] + j + 1)
                        if j >= 2:
                            pe.wait_ge(S["z_read"], s0["z_read"] + j - 1)
                        project(pe, l, IN_UNITS, T[j], ps_z[j % 2][:, :], j == 0, j == n - 1, S["z_done"])
                    j = st - 1
                    if 0 <= j < n:
                        pe.wait_ge(S["mix_a"], s0["mix_a"] + j + 1)
                        pe.wait_ge(S["mix_b"], s0["mix_b"] + j + 1)
                        if j:
                            pe.wait_ge(S["mix_lo"], s0["mix_lo"] + j)
                        else:
                            pe.wait_ge(ada_row, ADA_FIRST + ADA_TAIL * (l + 1) - ADA_LATE)
                        for k in range(KT):
                            mm = nc.tensor.transpose(ps_m[k // 4][:, (k % 4) * P:(k % 4 + 1) * P], X[:, T[j], k * P:(k + 1) * P], ident)
                        mm.then_inc(S["mixtr_done"], 1)
                for j, steps_now in enumerate(beside_ln1(l)):
                    if j < n:
                        pe.wait_ge(S["z_read"], s0["z_read"] + n + j - 1)
                        project(pe, l, IN_UNITS + 4, T[j], ps_z[j % 2][:, :], j == 0, j == n - 1, S["z_done"])
                    for i in steps_now:
                        transpose_step(l, 1, i)
                chunks = chunks_of(l)
                HB, YB, NY = 2 * len(chunks), 2 * n, share_banks(l)
                u0 = l * LAYER_UNITS + IN_UNITS + OUT_UNITS

                def hidden(b, ci, first):
                    t0, nt = chunks[ci]
                    for f in range(2):
                        j = 2 * ci + f
                        if ci == 0:
                            pe.wait_ge(w_ready, b * 4 + (u0 + f + 1))
                        if j >= 2 or not first:
                            pe.wait_ge(S["relu_done"], s0["relu_done"] + b * HB + (j - 1))
                        cols = slice(t0 * P, (t0 + nt) * P)
                        for k in range(KT):
                            wc = slice(k * P, (k + 1) * P)
                            o = banks[j % 2][:, 0:nt * P]
                            if first and f == 0:
                                pe.wait_ge(S["split_in"], s0["split_in"] + N_IN0 + KT * ci + k + 1)
                            nc.tensor.matmul(o, slot(mlp_slot(f), 0)[:, wc], x_hi[:, k, cols], start=k == 0, stop=False)
                            nc.tensor.matmul(o, slot(mlp_slot(f), 0)[:, wc], x_lo[:, k, cols], start=False, stop=False)
                            mm = nc.tensor.matmul(o, slot(mlp_slot(f), 1)[:, wc], x_hi[:, k, cols], start=False, stop=k == KT - 1)
                        mm.then_inc(S["h_done"], 1)

                def share(b, first):
                    for ti, t in enumerate(T):
                        for half in range(2):
                            yi = 2 * ti + half
                            if yi == 0:
                                pe.wait_ge(w_ready, b * 4 + (u0 + 4))
                            for ci, (t0, _) in enumerate(chunks):
                                if t == t0 and half == 0:
                                    pe.wait_ge(S["h_split"], s0["h_split"] + b * HB + 2 * (ci + 1))
                            if yi >= NY or not first:
                                pe.wait_ge(S["y_read"], s0["y_read"] + b * YB + (yi - NY + 1))
                            for f in range(2):
                                wc = slice(half * 512, (half + 1) * 512)
                                cols = slice(t * P, (t + 1) * P)
                                mm = three_passes(share_bank(l, yi)[:, :], h_hi[:, f, cols], h_lo[:, f, cols],
                                                  slot(mlp_slot(2 + f), 0)[:, wc], slot(mlp_slot(2 + f), 1)[:, wc], f == 0, f == 1)
                            mm.then_inc(S["y_done"], 1)

                for ci in range(len(chunks)):
                    if ci == len(chunks) - 1:
                        for i in range(KT * ci, KT * (ci + 1)):
                            transpose_step(l, 1, i)
                    hidden(0, ci, True)
                share(0, True)
                with pe.Fori(1, NBLK) as b:
                    for ci in range(len(chunks)):
                        hidden(b, ci, False)
                    share(b, False)

        @block.scalar
        def _(act):
            act.wait_ge(cond_in, 32)
            nc.scalar.activation(cond_s, cond, ACT.Silu).then_inc(cond_ready, 1)
            fetch(act, 0, unit_parts(0, 0))

            def normalise(l, ln, j):
                t = tiles_of(l)[j]
                act.wait_ge(S[ln + "_shift"], BEFORE[l][ln + "_shift"] + j + 1)
                nc.scalar.activation(X[:, t, :], X[:, t, :], ACT.Identity, bias=shift[:, j % 2, :], scale=rs[:, j % 2, :]).then_inc(S[ln + "_act"], 1)

            def load(l, u):
                split_high(act, l, u, next_unit(l, u))

            def modulate_step(l, which, j):
                s0, base = BEFORE[l], N_IN0 * which
                t0, n, k = in_chunks(l, which)[j]
                act.wait_ge(S["tr_in"], s0["tr_in"] + base + j + 1)
                if j >= 2:
                    act.wait_ge(S["split_in"], s0["split_in"] + base + j - 1)
                cd = cond_of(t0)
                nc.scalar.activation(mod32[:, j % 2, 0:n * P], tr_bank(which, j)[:, 0:n * P], ACT.Identity,
                                     bias=modc[:, 2 * which, cd, k:k + 1], scale=modc[:, 2 * which + 1, cd, k:k + 1]).then_inc(S["mod_in"], 1)

            for l in range(DEPTH):
                s0, T = BEFORE[l], tiles_of(l)
                n = len(T)
                act.wait_ge(S["one_added"], s0["one_added"] + 1)
                for j in range(N_IN0):
                    if j % 5 == 0 and j < 20:
                        load(l, j // 5)
                    modulate_step(l, 0, j)
                if l:
                    act.wait_ge(x_st, 32)
                act.wait_ge(S["split_in"], s0["split_in"] + N_IN0)
                steps, plan = PLANS[l]
                qn = [sum(st[0] == "Q" for st in steps[:i]) for i in range(len(steps) + 1)]
                R = len(conv_ranges(l))
                act.wait_ge(S["zero_set"], s0["zero_set"] + 1)
                for a in plan:
                    if a[0] == "load":
                        load(l, a[1])
                    elif a[0] == "masks":
                        act.wait_ge(S["small_in"], s0["small_in"] + 96)
                        nc.scalar.activation(decay, decay, ACT.Exp).then_inc(S["dec_op"], 1)
                        act.wait_ge(S["dec_op"], s0["dec_op"] + 1)
                        act.wait_ge(const_in, 32)
                        nc.scalar.activation(q_dec[:, :, 0], decay[:, 0, :], ACT.Exp, scale=expo[:, 0:1])
                        nc.scalar.activation(q_dec[:, :, 1], decay[:, 1, :], ACT.Exp, scale=expo[:, 1:2])
                        nc.scalar.activation(k_dec_raw[:, :, 0], decay[:, 0, :], ACT.Exp, scale=expo[:, 2:3])
                        nc.scalar.activation(k_dec_raw[:, :, 1], decay[:, 1, :], ACT.Exp, scale=expo[:, 3:4])
                        for h in range(2):
                            rows64 = slice(h * DK, (h + 1) * DK)
                            last = nc.scalar.activation(c_dec[rows64, :, :], decay[rows64, :, h::2], ACT.Exp, scale=-float(P))
                        last.then_inc(S["dec_op"], 1)
                        act.wait_ge(S["mask_arg"], s0["mask_arg"] + 1)
                        nc.scalar.activation(masks, masks, ACT.Exp).then_inc(S["mask_exp"], 1)
                    elif a[0] == "ada_load":
                        if a[1] % ADA_TAIL < ADA_BUFS:
                            act.wait_ge(S["proj_done"], s0["proj_done"] + len(steps) - NT + a[2])
                        else:
                            act.wait_ge(ada_row, a[1] - ADA_BUFS + 1)
                        ada_load(act, a[1])
                    elif a[0] == "ada_bias_load":
                        act.wait_ge(S["proj_done"], s0["proj_done"] + len(steps))
                        if a[1] % ADA_TAIL >= ADA_BUFS:
                            act.wait_ge(ada_row, a[1] - ADA_BUFS + 1)
                        ada_bias_load(act, a[1])
                    elif a[0] == "evac":
                        i = a[1]
                        kind, p, t = steps[i]
                        ps = ps_proj[i % 4]
                        act.wait_ge(S["proj_done"], s0["proj_done"] + i + 1)
                        if kind == "AB":
                            ab = i - qn[i]
                            if ab:
                                act.wait_ge(S["glu_done"], s0["glu_done"] + ab)
                            nc.scalar.activation(sig, ps[:, 2 * P:4 * P], ACT.Sigmoid).then_inc(S["sig_done"], 1)
                        else:
                            q = qn[i]
                            if q >= 2:
                                act.wait_ge(S["rot_done"], s0["rot_done"] + 2 * (q - 1))
                            nc.scalar.activation(qk_raw[:, q % 2, :], ps[:, 0:2 * P], ACT.Copy).then_inc(S["qk_ready"], 1)
                            if p:
                                act.wait_ge(S["vdec_done"], s0["vdec_done"] + q - NT + 1)
                                if t in T:
                                    act.wait_ge(S["val_done"], s0["val_done"] + row_of(l, p - 1, t) + 1)
                            nc.scalar.activation(v_sb[:, t, :], ps[:, 2 * P:3 * P], ACT.Copy).then_inc(S["v_ready"], 1)
                            if q >= 2:
                                act.wait_ge(S["g_st"][q % 2], s0["g_st"] + 16 * (q // 2))
                            nc.scalar.activation(g_out[:, q % 2, :], ps[:, 3 * P:4 * P], ACT.Copy).then_inc(S["evac_q"], 1)
                    elif a[0] == "post":
                        i = a[1]
                        kind, p, t = steps[i]
                        act.wait_ge(S["post_done"], s0["post_done"] + i + 1)
                        if kind == "AB":
                            if p:
                                act.wait_ge(S["conv_op"], s0["conv_op"] + 2 * TAPS * R)
                            at = REACH + t * P + (2 * REACH if t >= CTX_TILES else 0)
                            nc.scalar.activation(u_t[:, :, at:at + P], ps_tr[:, 0:2 * P].rearrange("p (a b) -> p a b", b=P), ACT.Copy).then_inc(S["post_evac"], 1)
                        else:
                            nc.scalar.activation(qk_t[:, t, :, :], ps_tr[:, 0:2 * P].rearrange("p (a b) -> p a b", b=P), ACT.Copy).then_inc(S["post_evac"], 1)
                            act.wait_ge(S["u_done"], s0["u_done"] + qn[i] + 1)
                            if p:
                                act.wait_ge(S["scan_op"], s0["scan_op"] + 2 * NT * p)
                            for h in range(2):
                                r64 = slice(h * DK, (h + 1) * DK)
                                last = nc.scalar.activation(kv_u[r64, t, :, :], ps_u[r64, h * P:(h + 1) * P].rearrange("p (a b) -> p a b", b=DK), ACT.Copy)
                            last.then_inc(S["u_evac"], 1)
                    elif a[0] == "scores":
                        _, p, t = a
                        r = row_of(l, p, t)
                        if r >= 2:
                            act.wait_ge(S["score_done"], s0["score_done"] + r - 1)
                        act.wait_ge(S["post_evac"], s0["post_evac"] + 1 + steps.index(("Q", p, t)))
                        for h in range(2):
                            r64 = slice(h * DK, (h + 1) * DK)
                            last = nc.scalar.activation(q_diag[r64, r % 2, h * P:(h + 1) * P], qk_t[r64, t, 0, :], ACT.Copy)
                        last.then_inc(S["qd_done"], 1)
                    elif a[0] == "values":
                        _, p, t = a
                        r = row_of(l, p, t)
                        act.wait_ge(S["scan_op"], s0["scan_op"] + 2 * NT * (p + 1))
                        if r >= 2:
                            act.wait_ge(S["val_done"], s0["val_done"] + r - 1)
                        for h in range(2):
                            r64 = slice(h * DK, (h + 1) * DK)
                            last = nc.scalar.activation(s_diag[r64, r % 2, h * P:(h + 1) * P].rearrange("p (a b) -> p a b", b=DK), state[r64, t, :, :], ACT.Copy)
                        last.then_inc(S["sd_done"], 1)
                for st in range(n + 2):
                    if st < n:
                        act.wait_ge(S["g_in"][st % 2], s0["g_in"] + 16 * (st // 2 + 1))
                        nc.scalar.activation(g_in[:, st % 2, :], g_in[:, st % 2, :], ACT.Silu).then_inc(S["silu_g"], 1)
                        act.wait_ge(S["gn_cent"], s0["gn_cent"] + st + 1)
                        if st:
                            act.wait_ge(S["gn_var"], s0["gn_var"] + st)
                        nc.scalar.activation(sq, X[:, T[st], 0:512], ACT.Square).then_inc(S["sq_done"], 1)
                        act.wait_ge(S["cn_shift"], s0["cn_shift"] + st + 1)
                        nc.scalar.activation(X[:, T[st], 512:D], banks[4 + st % 2][:, :], ACT.Identity,
                                             bias=shift[:, st % 2, :], scale=rs[:, st % 2, :]).then_inc(S["cnorm"], 1)
                    j = st - 1
                    if 0 <= j < n:
                        act.wait_ge(S["mixtr_done"], s0["mixtr_done"] + j + 1)
                        for half in range(2):
                            dst = x_hi[:, 4 * half:4 * half + 4, T[j] * P:(T[j] + 1) * P]
                            last = nc.scalar.activation(dst, banks[half][:, :].rearrange("p (a b) -> p a b", b=P), ACT.Copy)
                        last.then_inc(S["mix_hi"], 1)
                    if st < n:
                        act.wait_ge(S["conv_aff"], s0["conv_aff"] + st + 1)
                        nc.scalar.activation(X[:, T[st], 512:D], X[:, T[st], 512:D], ACT.Silu).then_inc(S["mix_b"], 1)
                    if st in (1, 2):
                        load(l, IN_UNITS + 3 + st)
                load(l, IN_UNITS + 6)
                load(l, IN_UNITS + 7)
                load(l, IN_UNITS + OUT_UNITS)
                load(l, IN_UNITS + OUT_UNITS + 1)
                act.wait_ge(S["one_added"], s0["one_added"] + 2)
                for turn, steps_now in enumerate(beside_ln1(l)):
                    if 1 <= turn <= n:
                        normalise(l, "ln", turn - 1)
                    for i in steps_now:
                        modulate_step(l, 1, i)
                chunks = chunks_of(l)
                HB, YB = 2 * len(chunks), 2 * n
                u0 = l * LAYER_UNITS + IN_UNITS + OUT_UNITS

                def hidden(b, j, first=False):
                    nt = chunks[j // 2][1]
                    act.wait_ge(S["h_done"], s0["h_done"] + b * HB + (j + 1))
                    if j >= 2 or not first:
                        act.wait_ge(S["h_sq"], s0["h_sq"] + b * HB + (j - 1))
                    nc.scalar.activation(relu[:, j % 2, 0:nt * P], banks[j % 2][:, 0:nt * P], ACT.Relu).then_inc(S["relu_done"], 1)

                def next_weights(b, next_fetches):
                    for sl, following in enumerate(next_fetches):
                        if sl == 2:
                            act.wait_ge(S["y_done"], s0["y_done"] + b * YB + YB)
                        un = u0 + 4 + sl
                        act.wait_ge(raw_in[un % 2], b * 64 + 32 * (un // 2 + 1))
                        nc.scalar.activation(slot(mlp_slot(sl), 0), raw[:, un % 2, :], ACT.Copy).then_inc(w_high, 1)
                        if following is not None:
                            act.wait_ge(w_ready, b * 4 + un)
                            fetch(act, (un + 1) % 2, following)

                def rest_of(b):
                    return [mlp_unit_parts(l, b, place) for place in (1, 2, 3)]

                for ci, (t0, nt) in enumerate(chunks):
                    if ci == 0:
                        load(l, IN_UNITS + OUT_UNITS + 2)
                    if ci == len(chunks) - 1:
                        for i in range(KT * ci, KT * (ci + 1)):
                            modulate_step(l, 1, i)
                        load(l, IN_UNITS + OUT_UNITS + 3)
                    hidden(0, 2 * ci, True)
                    hidden(0, 2 * ci + 1, True)
                    act.wait_ge(S["tr_in"], s0["tr_in"] + N_IN0 + KT * (ci + 1))
                    for t in range(t0, t0 + nt):
                        nc.scalar.activation(X[:, t, :], X[:, t, :], ACT.Copy, scale=ALPHA).then_inc(S["scaled"], 1)
                next_weights(0, [*rest_of(1), mlp_unit_parts(l, 2, 0)])
                with act.Fori(1, NBLK - 2) as b:
                    for j in range(HB):
                        hidden(b, j)
                    next_weights(b, [*rest_of(b + 1), mlp_unit_parts(l, b + 2, 0)])
                more = l + 1 < DEPTH
                for j in range(HB):
                    hidden(NBLK - 2, j)
                next_weights(NBLK - 2, [*rest_of(NBLK - 1), unit_parts(l + 1, 0) if more else None])
                for j in range(HB):
                    hidden(NBLK - 1, j)
                for j in range(n):
                    normalise(l, "ln2", j)

        @block.gpsimd
        def _(pool):
            nc.gpsimd.memset(neg_half, -0.5).then_inc(half_set, 1)
            pool.wait_ge(half_set, 1)

            for l in range(DEPTH):
                s0, T = BEFORE[l], tiles_of(l)
                n = len(T)
                for u in range(4):
                    split_low(pool, l, u)
                pool.wait_ge(S["split_in"], s0["split_in"] + N_IN0)
                if l:
                    pool.wait_ge(x_st, 32)
                nc.gpsimd.memset(diag_both, 0.0).then_inc(S["zero_set"], 1)
                steps, plan = PLANS[l]
                q = 0
                for a in plan:
                    if a[0] == "load":
                        split_low(pool, l, a[1])
                    elif a[0] == "evac" and steps[a[1]][0] == "Q":
                        _, p, t = steps[a[1]]
                        if q == 0:
                            pool.wait_ge(S["rope_in"], s0["rope_in"] + 32)
                            pool.wait_ge(S["kdec_done"], s0["kdec_done"] + 1)
                        pool.wait_ge(S["qk_ready"], s0["qk_ready"] + q + 1)
                        if q >= 2:
                            pool.wait_ge(S["u_done"], s0["u_done"] + q - 1)
                        src = qk_raw[:, q % 2, :].rearrange("p (h f e) -> p h f e", h=4, e=2)
                        dst = qk_rot[:, q % 2, :].rearrange("p (h f e) -> p h f e", h=4, e=2)
                        tmp = rot_tmp.rearrange("p (h f e) -> p h f e", h=4, e=2)
                        half = [P, 4, DK // 2]
                        cos = rope[:, t, 0, :].unsqueeze(1).to_broadcast(half)
                        sin = rope[:, t, 1, :].unsqueeze(1).to_broadcast(half)
                        if q:
                            pool.wait_ge(S["rot_done"], s0["rot_done"] + 2 * q)
                        for e in range(2):
                            nc.gpsimd.tensor_tensor(dst[:, :, :, e], src[:, :, :, e], cos, ALU.mult).then_inc(S["rot_part"], 1)
                            nc.gpsimd.tensor_tensor(tmp[:, :, :, e], src[:, :, :, 1 - e], sin, ALU.mult).then_inc(S["rot_part"], 1)
                        pool.wait_ge(S["rot_part"], s0["rot_part"] + 4 * (q + 1))
                        nc.gpsimd.tensor_tensor(dst[:, :, :, 0], dst[:, :, :, 0], tmp[:, :, :, 0], ALU.subtract).then_inc(S["rot_done"], 1)
                        nc.gpsimd.tensor_tensor(dst[:, :, :, 1], dst[:, :, :, 1], tmp[:, :, :, 1], ALU.add).then_inc(S["rot_done"], 1)
                        pool.wait_ge(S["v_ready"], s0["v_ready"] + q + 1)
                        if q:
                            pool.wait_ge(S["u_done"], s0["u_done"] + q)
                        kd = k_dec_raw if (l == DEPTH - 1 and t < CTX_TILES) else k_dec
                        by_head = [P, 2, 2, DK]
                        nc.gpsimd.tensor_tensor(v_dec.rearrange("p (h d e) -> p h d e", h=2, d=2),
                                                v_sb[:, t, :].rearrange("p (h e) -> p h e", h=2).unsqueeze(2).to_broadcast(by_head),
                                                kd[:, 2 * p:2 * p + 2, :].unsqueeze(3).to_broadcast(by_head), ALU.mult).then_inc(S["vdec_done"], 1)
                        q += 1
                for st in range(n + 1):
                    if st < n:
                        pool.wait_ge(S["cn_var"], s0["cn_var"] + st + 1)
                        nc.gpsimd.tensor_tensor(rs[:, st % 2, :], mv[:, st % 2, 1:2], neg_half[:, 0:1], ALU.pow).then_inc(S["cn_pow"], 1)
                        pool.wait_ge(S["gn_var"], s0["gn_var"] + st + 1)
                        nc.gpsimd.tensor_tensor(gstat[:, st % 2, 2 * HEADS:], gstat[:, st % 2, HEADS:2 * HEADS], neg_half[:, 0:HEADS], ALU.pow).then_inc(S["gn_pow"], 1)
                        o = X[:, T[st], 0:512]
                        if st == 0:
                            pool.wait_ge(S["rows_in"], s0["rows_in"] + 96)
                        pool.wait_ge(S["gn_norm"], s0["gn_norm"] + st + 1)
                        nc.gpsimd.tensor_tensor(o, o, rows[:, 0, :], ALU.mult).then_inc(S["gn_aff"], 1)
                        pool.wait_ge(S["gn_aff"], s0["gn_aff"] + 2 * st + 1)
                        nc.gpsimd.tensor_tensor(o, o, rows[:, 1, :], ALU.add).then_inc(S["gn_aff"], 1)
                        pool.wait_ge(S["gn_aff"], s0["gn_aff"] + 2 * st + 2)
                        pool.wait_ge(S["silu_g"], s0["silu_g"] + st + 1)
                        nc.gpsimd.tensor_tensor(o, o, g_in[:, st % 2, :], ALU.mult).then_inc(S["mix_a"], 1)
                    if st in (1, 2):
                        split_low(pool, l, IN_UNITS + 3 + st)
                for u in range(6, 10):
                    split_low(pool, l, IN_UNITS + u)

                def layer_norm_part(ln, done, ln_rows):
                    for st in range(n + 2):
                        if st < n:
                            pool.wait_ge(S[ln + "_var"], s0[ln + "_var"] + st + 1)
                            if st >= 2:
                                pool.wait_ge(S[ln + "_act"], s0[ln + "_act"] + st - 1)
                            nc.gpsimd.tensor_tensor(rs[:, st % 2, :], mv[:, st % 2, 1:2], neg_half[:, 0:1], ALU.pow).then_inc(S[ln + "_pow"], 1)
                        if st >= 2:
                            j = st - 2
                            xt = X[:, T[j], :]
                            if by_vector(ln, j):
                                pool.wait_ge(S[ln + "_x"], s0[ln + "_x"] + sum(by_vector(ln, i) for i in range(j + 1)))
                            else:
                                pool.wait_ge(S[ln + "_act"], s0[ln + "_act"] + j + 1)
                                nc.gpsimd.tensor_tensor(xt, xt, ln_rows[:, 0, :], ALU.mult).then_inc(S[ln + "_own"], 1)
                                pool.wait_ge(S[ln + "_own"], s0[ln + "_own"] + j // 2 + 1)
                            nc.gpsimd.tensor_tensor(xt, xt, ln_rows[:, 1, :], ALU.add).then_inc(done, 1)

                pool.wait_ge(S["gate_in"], s0["gate_in"] + 64)
                layer_norm_part("ln", S["ln1_done"], ln1_rows)
                for u in (2, 3):
                    split_low(pool, l, IN_UNITS + OUT_UNITS + u)
                u0 = l * LAYER_UNITS + IN_UNITS + OUT_UNITS

                def mlp_block(b, units):
                    for sl in range(units):
                        un = u0 + 4 + sl
                        pool.wait_ge(w_high, b * 4 + (un + 1))
                        nc.gpsimd.tensor_tensor(slot(mlp_slot(sl), 1), raw[:, un % 2, :], slot(mlp_slot(sl), 0).bitcast(F32), ALU.subtract).then_inc(w_ready, 1)

                with pool.Fori(0, NBLK - 1) as b:
                    mlp_block(b, 4)
                pool.wait_ge(S["gate2_in"], s0["gate2_in"] + 64)
                layer_norm_part("ln2", S["ln2_done"], ln2_rows)

        @block.vector
        def _(dve):
            chained = [0]

            def link(ins):
                chained[0] += 1
                ins.then_inc(dve_chain, 1)
                dve.wait_ge(dve_chain, chained[0])

            def ada_bias(g):
                dve.wait_ge(ada_done, g + 1)
                if g >= 2:
                    dve.wait_ge(ada_st[g % 2], 16 * (g // 2))
                nc.vector.tensor_tensor(ada_o[g % 2], ada_bank(g), ada_b[g % ADA_BUFS], ALU.add).then_inc(ada_row, 1)

            for g in range(ADA_FIRST):
                ada_bias(g)

            def split_step(l, which, j):
                s0, base = BEFORE[l], N_IN0 * which
                t0, n, k = in_chunks(l, which)[j]
                cols = slice(t0 * P, (t0 + n) * P)
                m32 = mod32[:, j % 2, 0:n * P]
                dve.wait_ge(S["mod_in"], s0["mod_in"] + base + j + 1)
                nc.vector.tensor_copy(x_hi[:, k, cols], m32).then_inc(S["hi_in"], 1)
                dve.wait_ge(S["hi_in"], s0["hi_in"] + base + j + 1)
                nc.vector.tensor_tensor(x_lo[:, k, cols], m32, x_hi[:, k, cols].bitcast(F32), ALU.subtract).then_inc(S["split_in"], 1)

            def row_stats(par, t, done):
                for half in range(2):
                    nc.vector.bn_stats(bn[:, par, 6 * half:6 * half + 6], X[:, t, half * 512:(half + 1) * 512]).then_inc(dve_chain, 1)
                chained[0] += 2
                dve.wait_ge(dve_chain, chained[0])
                link(nc.vector.bn_aggr(mv[:, par, :], bn[:, par, :]))
                nc.vector.tensor_scalar(mv[:, par, 1:2], mv[:, par, 1:2], EPS, None, ALU.add).then_inc(done, 1)

            def ln_shift(l, j, ln):
                dve.wait_ge(S[ln + "_pow"], BEFORE[l][ln + "_pow"] + j + 1)
                nc.vector.scalar_tensor_tensor(shift[:, j % 2, :], mv[:, j % 2, 0:1], -1.0, rs[:, j % 2, :], ALU.mult, ALU.mult).then_inc(S[ln + "_shift"], 1)

            def ln_weight(l, j, ln, ln_rows):
                if by_vector(ln, j):
                    dve.wait_ge(S[ln + "_act"], BEFORE[l][ln + "_act"] + j + 1)
                    xt = X[:, tiles_of(l)[j], :]
                    nc.vector.tensor_tensor(xt, xt, ln_rows[:, 0, :], ALU.mult).then_inc(S[ln + "_x"], 1)

            for l in range(DEPTH):
                s0, T = BEFORE[l], tiles_of(l)
                n = len(T)
                dve.wait_ge(S["small_in"], s0["small_in"] + 96)
                nc.vector.tensor_scalar(modc[:, 1, :, :], modc[:, 1, :, :], 1.0, None, ALU.add).then_inc(S["one_added"], 1)
                for j in range(N_IN0):
                    split_step(l, 0, j)
                if l:
                    dve.wait_ge(x_st, 32)
                nc.vector.memset(u_t[:, :, 0:REACH], 0.0)
                mid = REACH + CTX_TILES * P
                nc.vector.memset(u_t[:, :, mid:mid + 2 * REACH], 0.0)
                link(nc.vector.memset(u_t[:, :, UT - REACH:UT], 0.0))
                steps, plan = PLANS[l]
                qn = [sum(st[0] == "Q" for st in steps[:i]) for i in range(len(steps) + 1)]
                runs = conv_ranges(l)
                R = len(runs)
                F_ORDER = list(range(NT))
                B_ORDER = [1, 0] + list(range(NT - 1, CTX_TILES - 1, -1))
                for a in plan:
                    if a[0] == "evac" and steps[a[1]][0] == "AB":
                        i = a[1]
                        ab = i - qn[i]
                        dve.wait_ge(S["sig_done"], s0["sig_done"] + ab + 1)
                        if ab >= 2:
                            prev = [k for k in range(i) if steps[k][0] == "AB"][ab - 2]
                            dve.wait_ge(S["post_done"], s0["post_done"] + prev + 1)
                        nc.vector.tensor_tensor(u_sb[:, ab % 2, :], ps_proj[i % 4][:, 0:2 * P], sig, ALU.mult).then_inc(S["glu_done"], 1)
                    elif a[0] == "ada_row":
                        ada_bias(a[1])
                    elif a[0] == "masks":
                        dve.wait_ge(S["rope_in"], s0["rope_in"] + 32)
                        dve.wait_ge(S["dec_op"], s0["dec_op"] + 2)
                        nc.vector.tensor_scalar(k_dec, k_dec_raw, K_SCALE, None, ALU.mult).then_inc(S["kdec_done"], 1)
                        link(nc.vector.tensor_scalar(ident_s, ident, K_SCALE, None, ALU.mult))
                        for h in range(HEADS):
                            link(nc.vector.tensor_scalar(masks[:, h, :], dist[:, 1, :], decay[:, 1, h:h + 1], None, ALU.mult))
                            last = nc.vector.scalar_tensor_tensor(masks[:, h, :], dist[:, 0, :], decay[:, 0, h:h + 1], masks[:, h, :], ALU.mult, ALU.add)
                            if h < HEADS - 1:
                                link(last)
                        last.then_inc(S["mask_arg"], 1)
                        dve.wait_ge(S["mask_exp"], s0["mask_exp"] + 1)
                        link(nc.vector.scalar_tensor_tensor(masks, masks, K_SCALE, ident_s.unsqueeze(1).to_broadcast([P, HEADS, P]), ALU.mult, ALU.add))
                    elif a[0] == "scan":
                        p = a[1]
                        base = 2 * NT * p
                        dve.wait_ge(S["u_evac"], s0["u_evac"] + NT * (p + 1))
                        if p:
                            dve.wait_ge(S["sd_done"], s0["sd_done"] + n * p)
                        nc.vector.memset(state[:, F_ORDER[0], 0, :], 0.0).then_inc(S["scan_op"], 1)
                        nc.vector.memset(state[:, B_ORDER[0], 1, :], 0.0).then_inc(S["scan_op"], 1)
                        for k in range(1, NT):
                            for d, order in enumerate((F_ORDER, B_ORDER)):
                                dve.wait_ge(S["scan_op"], s0["scan_op"] + base + 2 * k + d - 1)
                                nc.vector.scalar_tensor_tensor(state[:, order[k], d, :], state[:, order[k - 1], d, :], c_dec[:, d, p:p + 1],
                                                               kv_u[:, order[k - 1], d, :], ALU.mult, ALU.add).then_inc(S["scan_op"], 1)
                    elif a[0] == "scores":
                        _, p, t = a
                        r = row_of(l, p, t)
                        dve.wait_ge(S["score_done"], s0["score_done"] + r + 1)
                        if r >= 2:
                            dve.wait_ge(S["val_done"], s0["val_done"] + r - 1)
                        nc.vector.tensor_tensor(probs[:, r % 2, :], ps_sc[:, 0:2 * P], masks[:, 2 * p:2 * p + 2, :].rearrange("p a b -> p (a b)"), ALU.mult).then_inc(S["prob_done"], 1)
                    elif a[0] == "values":
                        _, p, t = a
                        r = row_of(l, p, t)
                        dve.wait_ge(S["val_done"], s0["val_done"] + r + 1)
                        if r:
                            dve.wait_ge(S["comb_done"], s0["comb_done"] + r)
                        by_dir = inter.rearrange("p (h d e) -> p h d e", h=2, d=2)
                        nc.vector.tensor_tensor(inter.rearrange("p (a e) -> p a e", e=DK), ps_o[:, P:3 * P].rearrange("p (a e) -> p a e", e=DK),
                                                q_dec[:, 2 * p:2 * p + 2, :].rearrange("p a b -> p (a b)").unsqueeze(2).to_broadcast([P, 4, DK]), ALU.mult).then_inc(S["comb_a"], 1)
                        dve.wait_ge(S["comb_a"], s0["comb_a"] + r + 1)
                        nc.vector.tensor_tensor(by_dir[:, :, 0, :], ps_o[:, 0:P].rearrange("p (h e) -> p h e", h=2),
                                                by_dir[:, :, 0, :], ALU.add).then_inc(S["comb_b"], 1)
                        dve.wait_ge(S["comb_b"], s0["comb_b"] + r + 1)
                        if r >= 2:
                            dve.wait_ge(S["o_st"][r % 2], s0["o_st"] + 16 * (r // 2))
                        nc.vector.tensor_tensor(o_out[:, r % 2, :].rearrange("p (h e) -> p h e", h=2), by_dir[:, :, 0, :],
                                                by_dir[:, :, 1, :], ALU.add).then_inc(S["comb_done"], 1)
                    elif a[0] == "taps":
                        _, h, a0, a1 = a
                        if (h, a0) == (0, 0):
                            dve.wait_ge(S["conv_in"], s0["conv_in"] + 80)
                        if a0 == 0:
                            dve.wait_ge(S["post_evac"], s0["post_evac"] + 1 + max(k for k, st in enumerate(steps) if st[:2] == ("AB", h)))
                        for k in range(a0, a1):
                            ct, tap = k // TAPS, k % TAPS
                            if tap == 0 and h + ct:
                                dve.wait_ge(S["cv_st"], s0["cv_st"] + 16 * (2 * h + ct))
                            for r, (at, w, src) in enumerate(runs):
                                taps_in = u_t[:, ct, src + tap:src + tap + w]
                                wcol = cw[:, 2 * h + ct, tap:tap + 1]
                                if tap == 0:
                                    nc.vector.tensor_scalar(acc[:, at:at + w], taps_in, wcol, cb[:, 2 * h + ct:2 * h + ct + 1], ALU.mult, ALU.add).then_inc(S["conv_op"], 1)
                                else:
                                    dve.wait_ge(S["conv_op"], s0["conv_op"] + ((h * 2 * TAPS) + k) * R + r - R + 1)
                                    nc.vector.scalar_tensor_tensor(acc[:, at:at + w], taps_in, wcol, acc[:, at:at + w], ALU.mult, ALU.add).then_inc(S["conv_op"], 1)
                for st in range(n + 3):
                    if st < n:
                        t, par = T[st], st % 2
                        ps = banks[4 + par]
                        o = X[:, t, 0:512].rearrange("p (h e) -> p h e", h=HEADS)
                        xc = X[:, t, 512:D]
                        mean, var, rstd = (gstat[:, par, i * HEADS:(i + 1) * HEADS] for i in range(3))
                        dve.wait_ge(S["cvt_done"], s0["cvt_done"] + st + 1)
                        link(nc.vector.bn_stats(bn[:, par, 0:6], ps[:, :]))
                        link(nc.vector.bn_aggr(mv[:, par, :], bn[:, par, 0:6]))
                        nc.vector.tensor_scalar(mv[:, par, 1:2], mv[:, par, 1:2], EPS, None, ALU.add).then_inc(S["cn_var"], 1)
                        dve.wait_ge(S["o_in"][par], s0["o_in"] + 16 * (st // 2 + 1))
                        link(nc.vector.tensor_reduce(mean, o, AX.X, ALU.add))
                        link(nc.vector.tensor_scalar(mean, mean, 1.0 / DK, None, ALU.mult))
                        nc.vector.tensor_tensor(o, o, mean.unsqueeze(2).to_broadcast([P, HEADS, DK]), ALU.subtract).then_inc(S["gn_cent"], 1)
                        dve.wait_ge(S["cn_pow"], s0["cn_pow"] + st + 1)
                        nc.vector.scalar_tensor_tensor(shift[:, par, :], mv[:, par, 0:1], -1.0, rs[:, par, :], ALU.mult, ALU.mult).then_inc(S["cn_shift"], 1)
                        dve.wait_ge(S["sq_done"], s0["sq_done"] + st + 1)
                        link(nc.vector.tensor_reduce(var, sq.rearrange("p (h e) -> p h e", h=HEADS), AX.X, ALU.add))
                        nc.vector.tensor_scalar(var, var, 1.0 / DK, EPS, ALU.mult, ALU.add).then_inc(S["gn_var"], 1)
                        if st == 0:
                            dve.wait_ge(S["rows_in"], s0["rows_in"] + 96)
                        dve.wait_ge(S["cnorm"], s0["cnorm"] + st + 1)
                        link(nc.vector.tensor_tensor(xc, xc, rows[:, 2, :], ALU.mult))
                        nc.vector.tensor_tensor(xc, xc, rows[:, 3, :], ALU.add).then_inc(S["conv_aff"], 1)
                        dve.wait_ge(S["gn_pow"], s0["gn_pow"] + st + 1)
                        nc.vector.tensor_tensor(o, o, rstd.unsqueeze(2).to_broadcast([P, HEADS, DK]), ALU.mult).then_inc(S["gn_norm"], 1)
                    if 1 <= st <= ADA_LATE:
                        ada_bias(ADA_FIRST + ADA_TAIL * (l + 1) - ADA_LATE + st - 1)
                    j = st - 3
                    if j >= 0:
                        dve.wait_ge(S["z_done"], s0["z_done"] + j + 1)
                        dve.wait_ge(S["res_in"][j % 2], s0["res_in"] + 16 * (j // 2 + 1))
                        nc.vector.tensor_tensor(z_t, banks[2 + j % 2][:, :], gate_row[:, cond_of(T[j]), :], ALU.mult).then_inc(S["z_read"], 1)
                        dve.wait_ge(S["z_read"], s0["z_read"] + j + 1)
                        link(nc.vector.scalar_tensor_tensor(X[:, T[j], 0:512], X[:, T[j], 0:512], ALPHA, z_t, ALU.mult, ALU.add))
                    j = st - 1
                    if 0 <= j < n:
                        dve.wait_ge(S["mix_hi"], s0["mix_hi"] + j + 1)
                        cols = slice(T[j] * P, (T[j] + 1) * P)
                        for half in range(2):
                            last = nc.vector.tensor_tensor(x_lo[:, 4 * half:4 * half + 4, cols], banks[half][:, :].rearrange("p (a b) -> p a b", b=P),
                                                           x_hi[:, 4 * half:4 * half + 4, cols].bitcast(F32), ALU.subtract)
                        last.then_inc(S["mix_lo"], 1)
                dve.wait_ge(S["gate_in"], s0["gate_in"] + 64)
                dve.wait_ge(S["mod2_in"], s0["mod2_in"] + 64)
                nc.vector.tensor_scalar(modc[:, 3, :, :], modc[:, 3, :, :], 1.0, None, ALU.add).then_inc(S["one_added"], 1)
                for st, steps_now in enumerate(beside_ln1(l)):
                    if st < n:
                        dve.wait_ge(S["z_done"], s0["z_done"] + n + st + 1)
                        nc.vector.tensor_tensor(z_t, banks[2 + st % 2][:, :], g_in[:, cond_of(T[st]), :], ALU.mult).then_inc(S["z_read"], 1)
                        dve.wait_ge(S["z_read"], s0["z_read"] + n + st + 1)
                        link(nc.vector.scalar_tensor_tensor(X[:, T[st], 512:D], X[:, T[st], 512:D], ALPHA, z_t, ALU.mult, ALU.add))
                        row_stats(st % 2, T[st], S["ln_var"])
                    if 1 <= st <= n:
                        ln_shift(l, st - 1, "ln")
                    if st >= 2:
                        ln_weight(l, st - 2, "ln", ln1_rows)
                    for i in steps_now:
                        split_step(l, 1, i)
                chunks = chunks_of(l)
                HB, YB = 2 * len(chunks), 2 * n

                def hidden(b, j, first):
                    t0, nt = chunks[j // 2]
                    cols = slice(t0 * P, (t0 + nt) * P)
                    w = nt * P
                    a32 = act32[:, j % 2, 0:w]
                    dve.wait_ge(S["relu_done"], s0["relu_done"] + b * HB + (j + 1))
                    if j >= 2 or not first:
                        dve.wait_ge(S["h_split"], s0["h_split"] + b * HB + (j - 1))
                    rl = relu[:, j % 2, 0:w]
                    nc.vector.tensor_tensor(a32, rl, rl, ALU.mult).then_inc(S["h_sq"], 1)
                    dve.wait_ge(S["h_sq"], s0["h_sq"] + b * HB + (j + 1))
                    if j == 0 and not first:
                        dve.wait_ge(S["y_done"], s0["y_done"] + b * YB)
                    nc.vector.tensor_copy(h_hi[:, j % 2, cols], a32).then_inc(S["h_high"], 1)
                    dve.wait_ge(S["h_high"], s0["h_high"] + b * HB + (j + 1))
                    nc.vector.tensor_tensor(h_lo[:, j % 2, cols], a32, h_hi[:, j % 2, cols].bitcast(F32), ALU.subtract).then_inc(S["h_split"], 1)

                def share(b, first, last=False):
                    for ti, t in enumerate(T):
                        if first:
                            if ti == 0:
                                dve.wait_ge(S["gate2_in"], s0["gate2_in"] + 32)
                            dve.wait_ge(S["scaled"], s0["scaled"] + ti + 1)
                        for half in range(2):
                            yi = 2 * ti + half
                            hc = slice(half * 512, (half + 1) * 512)
                            dve.wait_ge(S["y_done"], s0["y_done"] + b * YB + (yi + 1))
                            if yi >= 2 or not first:
                                dve.wait_ge(S["y_add"], s0["y_add"] + b * YB + (yi - 1))
                            nc.vector.tensor_tensor(y_t[:, yi % 2, :], share_bank(l, yi)[:, :], gate2[:, cond_of(t), hc], ALU.mult).then_inc(S["y_read"], 1)
                            dve.wait_ge(S["y_read"], s0["y_read"] + b * YB + (yi + 1))
                            nc.vector.tensor_tensor(X[:, t, hc], X[:, t, hc], y_t[:, yi % 2, :], ALU.add).then_inc(S["y_add"], 1)
                        if last:
                            dve.wait_ge(S["y_add"], s0["y_add"] + b * YB + 2 * (ti + 1))
                            row_stats(ti % 2, t, S["ln2_var"])
                            if ti >= 1:
                                ln_shift(l, ti - 1, "ln2")
                            if ti == 2:
                                dve.wait_ge(S["gate2_in"], s0["gate2_in"] + 64)
                            if ti >= 2:
                                ln_weight(l, ti - 2, "ln2", ln2_rows)

                for ci in range(len(chunks)):
                    if ci == len(chunks) - 1:
                        for i in range(KT * ci, KT * (ci + 1)):
                            split_step(l, 1, i)
                    hidden(0, 2 * ci, True)
                    hidden(0, 2 * ci + 1, True)
                share(0, True)
                with dve.Fori(1, NBLK - 1) as b:
                    for j in range(HB):
                        hidden(b, j, False)
                    share(b, False)
                for j in range(HB):
                    hidden(NBLK - 1, j, False)
                share(NBLK - 1, False, last=True)
                ln_shift(l, n - 1, "ln2")
                ln_weight(l, n - 2, "ln2", ln2_rows)
                ln_weight(l, n - 1, "ln2", ln2_rows)


INPUTS = ["x", "c", "ctx", "c_ctx", "w_ada", "b_ada", "w_in", "ret_log_rate_fwd", "ret_log_rate_bwd",
          "ret_gn_w", "ret_gn_b", "conv_w", "conv_b", "conv_ln_w", "conv_ln_b", "w_out", "ln1_w", "ln1_b",
          "w_ff1", "w_ff2", "ln2_w", "ln2_b"]


def kernel(**inputs):
    import concourse.bacc as bacc
    from concourse.bass_utils import run_bass_kernel_spmd

    nc = bacc.Bacc("TRN2", target_bir_lowering=False, num_devices=1)
    arrays = {name: np.ascontiguousarray(inputs[name]) for name in INPUTS}
    arrays.update(shape_constants())
    args = [nc.dram_tensor(f"in_{name}", a.shape, mybir.dt.from_np(a.dtype), kind="ExternalInput").ap() for name, a in arrays.items()]
    out = nc.dram_tensor("out", (1, LAT_TILES * P, D), F32, kind="ExternalOutput").ap()
    build(nc, *args, out)
    result = run_bass_kernel_spmd(nc, [{f"in_{name}": a for name, a in arrays.items()}], core_ids=[0])
    return result.results[0]["out"]
```
